# Optimizing a Trainium2 kernel written in Bass

```python
import math
import jax, jax.numpy as jnp
from jax import lax
import numpy as np

"""Bidirectional hybrid encoder trunk: DEPTH layers, each a sandwich-normed
parallel-branch token-mixing block (short gated conv + differential attention
with ALiBi, merged by per-channel sigmoid gates, one output projection)
followed by a sandwich-normed squared-ReLU MLP.
Input  x: (BATCH, SEQ, D_MODEL) float32.
Output  : (BATCH, SEQ, D_MODEL).
"""

D_MODEL = 1024
BATCH = 1
SEQ = 1024
DEPTH = 1

CONV_WIDTH = D_MODEL // 2
CONV_K = 3
N_HEADS = 4
HEAD_DIM = D_MODEL // 16
V_DIM = 2 * HEAD_DIM
ATTN_WIDTH = N_HEADS * V_DIM
N_BRANCH = 2
D_FF = 4 * D_MODEL
Q_BLOCK = 128
EPS = 1e-6
IN_WIDTH = 3 * CONV_WIDTH + 3 * ATTN_WIDTH + N_BRANCH * D_MODEL

kernel_name = "hybrid_shortconv_diffattn_alibi_encoder"

def rmsnorm(x, g):
    xf = x.astype(jnp.float32)
    y = xf * lax.rsqrt(jnp.mean(xf * xf, axis=-1, keepdims=True) + EPS)
    return (y * g.astype(jnp.float32)).astype(x.dtype)

def alibi_slopes():
    i = jnp.arange(1, N_HEADS + 1, dtype=jnp.float32)
    return jnp.exp2(-8.0 * i / N_HEADS)

def diff_attention(q1, q2, k1, k2, v, lam):
    b, h, s, _ = q1.shape
    nb = s // Q_BLOCK
    scale = HEAD_DIM ** -0.5
    slopes = alibi_slopes()
    kpos = jnp.arange(s, dtype=jnp.float32)

    def to_blocks(q):
        return q.reshape(b, h, nb, Q_BLOCK, HEAD_DIM).transpose(2, 0, 1, 3, 4)

    starts = jnp.arange(nb, dtype=jnp.int32) * Q_BLOCK

    def block(args):
        q1b, q2b, start = args
        qpos = (start + jnp.arange(Q_BLOCK, dtype=jnp.int32)).astype(jnp.float32)
        bias = -slopes[:, None, None] * jnp.abs(qpos[:, None] - kpos[None, :])
        s1 = jnp.einsum('bhqd,bhkd->bhqk', q1b, k1).astype(jnp.float32) * scale + bias
        s2 = jnp.einsum('bhqd,bhkd->bhqk', q2b, k2).astype(jnp.float32) * scale + bias
        a = jax.nn.softmax(s1, axis=-1) - lam * jax.nn.softmax(s2, axis=-1)
        return jnp.einsum('bhqk,bhkv->bhqv', a.astype(v.dtype), v)

    o = lax.map(block, (to_blocks(q1), to_blocks(q2), starts))
    return o.transpose(1, 2, 0, 3, 4).reshape(b, h, s, V_DIM)

def mixing_block(u, w_in, b_gate, conv_w, w_conv_out, lambda_qk, subln_g,
                 w_attn_out, w_o, lam_init):
    b, s, _ = u.shape
    proj = u @ w_in
    cw, aw = CONV_WIDTH, ATTN_WIDTH
    offs = [cw, 2 * cw, 3 * cw, 3 * cw + aw, 3 * cw + 2 * aw, 3 * cw + 3 * aw]
    hc, bc, cc, q, k, v, gates = jnp.split(proj, offs, axis=-1)

    inner = cc * hc
    pad = jnp.pad(inner, ((0, 0), (CONV_K // 2, CONV_K // 2), (0, 0)))
    conv = pad[:, 0:s] * conv_w[0]
    for tap in range(1, CONV_K):
        conv = conv + pad[:, tap:tap + s] * conv_w[tap]
    y_conv = (bc * conv) @ w_conv_out

    q = q.reshape(b, s, N_HEADS, 2, HEAD_DIM)
    k = k.reshape(b, s, N_HEADS, 2, HEAD_DIM)
    q1 = q[:, :, :, 0].transpose(0, 2, 1, 3)
    q2 = q[:, :, :, 1].transpose(0, 2, 1, 3)
    k1 = k[:, :, :, 0].transpose(0, 2, 1, 3)
    k2 = k[:, :, :, 1].transpose(0, 2, 1, 3)
    vh = v.reshape(b, s, N_HEADS, V_DIM).transpose(0, 2, 1, 3)
    lq = lambda_qk.astype(jnp.float32)
    lam = (jnp.exp(jnp.sum(lq[0] * lq[1])) - jnp.exp(jnp.sum(lq[2] * lq[3]))
           + lam_init)
    o = diff_attention(q1, q2, k1, k2, vh, lam)
    o = rmsnorm(o, subln_g) * (1.0 - lam_init)
    o = o.transpose(0, 2, 1, 3).reshape(b, s, ATTN_WIDTH)
    y_attn = o @ w_attn_out

    g = jax.nn.sigmoid((gates + b_gate.reshape(-1)).astype(jnp.float32))
    g = g.reshape(b, s, N_BRANCH, D_MODEL)
    merged = (g[:, :, 0] * y_conv + g[:, :, 1] * y_attn).astype(u.dtype)
    return merged @ w_o

def setup_inputs(seed: int = 0) -> dict:
    key = jax.random.key(seed)
    ks = jax.random.split(key, 12)
    f32 = jnp.float32
    n = lambda k, shp: jax.random.normal(k, shp, dtype=f32)
    return {
        "x": n(ks[0], (BATCH, SEQ, D_MODEL)),
        "w_in": n(ks[1], (DEPTH, D_MODEL, IN_WIDTH)) * D_MODEL ** -0.5,
        "b_gate": 0.01 * n(ks[2], (DEPTH, N_BRANCH, D_MODEL)),
        "conv_w": n(ks[3], (DEPTH, CONV_K, CONV_WIDTH)) * CONV_K ** -0.5,
        "w_conv_out": n(ks[4], (DEPTH, CONV_WIDTH, D_MODEL)) * CONV_WIDTH ** -0.5,
        "lambda_qk": 0.1 * n(ks[5], (DEPTH, 4, HEAD_DIM)),
        "subln_g": 1.0 + 0.02 * n(ks[6], (DEPTH, V_DIM)),
        "w_attn_out": n(ks[7], (DEPTH, ATTN_WIDTH, D_MODEL)) * ATTN_WIDTH ** -0.5,
        "w_o": n(ks[8], (DEPTH, D_MODEL, D_MODEL)) * D_MODEL ** -0.5,
        "norm_g": 1.0 + 0.02 * n(ks[9], (DEPTH, 4, D_MODEL)),
        "w_ff1": n(ks[10], (DEPTH, D_MODEL, D_FF)) * D_MODEL ** -0.5,
        "w_ff2": n(ks[11], (DEPTH, D_FF, D_MODEL)) * D_FF ** -0.5,
    }

def reference(x, w_in, b_gate, conv_w, w_conv_out, lambda_qk, subln_g,
              w_attn_out, w_o, norm_g, w_ff1, w_ff2):
    h = x
    for l in range(DEPTH):
        lam_init = 0.8 - 0.6 * math.exp(-0.3 * l)
        u = rmsnorm(h, norm_g[l, 0])
        m = mixing_block(u, w_in[l], b_gate[l], conv_w[l], w_conv_out[l],
                         lambda_qk[l], subln_g[l], w_attn_out[l], w_o[l], lam_init)
        h = h + rmsnorm(m, norm_g[l, 1])
        u = rmsnorm(h, norm_g[l, 2])
        f = jnp.square(jax.nn.relu(u @ w_ff1[l])) @ w_ff2[l]
        h = h + rmsnorm(f, norm_g[l, 3])
    return h


_drawn_inputs = setup_inputs


def setup_inputs(seed=0):
    import zlib

    import numpy as np

    out = dict(_drawn_inputs(seed))
    spreads = {}
    factors = {'b_gate': 8.0, 'subln_g': 5.575}
    for name, (base, spread) in spreads.items():
        noise = np.random.default_rng([zlib.crc32(name.encode()), seed]).standard_normal(out[name].shape)
        drawn = base * np.exp(spread * noise) if base else spread * noise
        out[name] = __import__('jax').numpy.asarray(drawn.astype(out[name].dtype))
    for name, factor in factors.items():
        out[name] = (out[name] * factor).astype(out[name].dtype)
    return out
```

```python
from contextlib import ExitStack

import concourse.bass as bass
from concourse import mybir

ALU = mybir.AluOpType
ACT = mybir.ActivationFunctionType
F32 = mybir.dt.float32
F32R = mybir.dt.float32r

P = 128
D = 1024
S = 1024
KT = D // P
TT = S // P
HALF = 512
NH = S // HALF
CONV_K = 3
CT = D // 2 // P
HEADS = 4
HD = D // 16
QB = S // P
FF = 4 * D
FFC = 4
CHUNKS = FF // P // FFC
EPS = 1e-6
LAM_INIT = 0.8 - 0.6
SCALE = HD ** -0.5
SLOPES = [2.0 ** (-8.0 * (h + 1) / HEADS) for h in range(HEADS)]
RING = 2

PAR_G = 0
PAR_B = PAR_G + 4 * KT
PAR_C = PAR_B + 2 * KT
PAR_S = PAR_C + CONV_K * CT
NPAR = PAR_S + 1

COL_H, COL_B, COL_C = 0, CT * P, 2 * CT * P
COL_Q = 3 * CT * P
COL_K = COL_Q + HEADS * P
COL_V = COL_K + HEADS * P
COL_G = COL_V + HEADS * P

OPENING = [("q", 0), ("q", 1), ("k", 0), ("k", 1)]
OPENING_WITH_TAIL = [("q", 0), ("C", 7), ("q", 1), ("T", 7), ("k", 0), ("AV", 1), ("k", 1)]
REST = [("v", 0), ("v", 1), ("S", 0), ("M", 0), ("h", 0), ("C", 0), ("VT", 0), ("S", 1), ("h", 1), ("T", 0),
        ("M", 1), ("c", 0), ("C", 1), ("S", 2), ("c", 1), ("T", 1), ("M", 2), ("b", 0), ("C", 2), ("S", 3),
        ("b", 1), ("T", 2), ("M", 3), ("g", 0), ("C", 3), ("S", 4), ("g", 1), ("T", 3), ("M", 4), ("g", 2),
        ("AV", 0), ("C", 4), ("S", 5), ("g", 3), ("T", 4), ("M", 5), ("g", 4), ("C", 5), ("S", 6), ("g", 5),
        ("T", 5), ("M", 6), ("g", 6), ("C", 6), ("S", 7), ("g", 7), ("T", 6), ("M", 7)]
TAIL = [("C", 7), ("T", 7), ("AV", 1)]
PANELS = ["q", "k", "v", "h", "c", "b", "g"]
HEAD_PANELS = 10
HEAD_UNITS = 2 * HEAD_PANELS
TB_USES = 11
TB = {("VT", 0): 0, ("AV", 0): 5, ("AV", 1): 10}
TB.update({("T", t): 1 + t + (t > 3) for t in range(QB)})

PASSES = ((0, 0), (0, 1), (1, 0))


def unit_of(kind, n):
    return 2 * PANELS.index(kind) + n


def tb_use(i, kind, n):
    return i * TB_USES + (TB[kind, n] - (TB_USES if (kind, n) in (("T", 7), ("AV", 1)) else 0))


def one(ap, i):
    return ap[:, bass.ds(i, 1)].rearrange("p o c -> p (o c)")


def build(nc, x, w_in, b_gate, conv_w, w_conv_out, lambda_qk, subln_g, w_attn_out, w_o, norm_g,
          w_ff1, w_ff2, out):
    ctx = ExitStack()

    def sb(name, shape, dt=F32, scope=None):
        return (scope or ctx).enter_context(nc.sbuf_tensor(name, shape, dt))

    def sem(name):
        return ctx.enter_context(nc.semaphore(name))

    with ctx:
        act_hl = [sb("act_hi", [P, KT, S], F32R), sb("act_lo", [P, KT, S], F32R)]
        w_raw = [sb(f"w_raw{s}", [P, KT, P]) for s in range(RING)]
        w_hl = [[sb(f"w_hi{s}", [P, KT, P], F32R), sb(f"w_lo{s}", [P, KT, P], F32R)] for s in range(RING)]
        ident = sb("ident", [P, P])
        ones = sb("ones", [P, P])
        par = sb("par", [P, NPAR + 2])
        bhalf = sb("bhalf", [P, 2 * KT])
        gate_bias = sb("gate_bias", [P, 4])
        stats = sb("stats", [P, 2 * TT])
        small = sb("small", [P, 20])
        neg_lam = par[:, NPAR:NPAR + 1]
        sub_gain = par[:, NPAR + 1:NPAR + 2]
        neg_max, exp_sum, recip = small[:, 0:2], small[:, 2:4], small[:, 4:6]
        weight2, eps, spare, maxima = small[:, 6:7], small[:, 7:8], small[:, 8:9], small[:, 10:12]
        dots, dot_exp, lam_diff = small[:, 12:14], small[:, 14:16], small[:, 16:17]

        with ExitStack() as scope:
            z = sb("z", [P, CT, S], scope=scope)
            o = sb("o", [P, HEADS, S], scope=scope)
            with ExitStack() as loop_scope:
                table = sb("alibi", [P, 2 * S - P], scope=loop_scope)
                inner = sb("inner", [P, S + 2], scope=loop_scope)
                with ExitStack() as s1:
                    xn = sb("xn", [P, TT, D], scope=s1)
                    xsq = sb("xsq", [P, D], scope=s1)
                    par_rows = sb("par_rows", [NPAR, P], scope=s1)
                    lqk = sb("lqk", [P, 4, HD], scope=s1)
                    lq_junk = sb("lq_junk", [P, HD], scope=s1)
                with ExitStack() as s2:
                    q_hl = [sb("q_hi", [P, S], F32R, s2), sb("q_lo", [P, S], F32R, s2)]
                    k_hl = [sb("k_hi", [P, S], F32R, s2), sb("k_lo", [P, S], F32R, s2)]
                    vt = sb("vt", [P, S], scope=s2)
                    v_hl = [sb("v_hi", [P, TT, P], F32R, s2), sb("v_lo", [P, TT, P], F32R, s2)]
                    e = [sb(f"e{c}", [P, S], scope=s2) for c in range(2)]
                    at_hl = [sb("at_hi", [P, TT, HALF], F32R, s2), sb("at_lo", [P, TT, HALF], F32R, s2)]
                    gate_out = [sb(f"gate_out{s}", [P, HALF], scope=s2) for s in range(2)]
            with ExitStack() as s3:
                z_hl = [sb("z_hi", [P, CT, S], F32R, s3), sb("z_lo", [P, CT, S], F32R, s3)]
                o_hl = [sb("o_hi", [P, HEADS, S], F32R, s3), sb("o_lo", [P, HEADS, S], F32R, s3)]
                gate_in = [sb(f"gate_in{s}", [P, 2, HALF], scope=s3) for s in range(2)]
                prod = [sb(f"prod{s}", [P, HALF], scope=s3) for s in range(3)]
                osq = [sb(f"osq{s}", [P, HALF], scope=s3) for s in range(2)]
                odev = sb("odev", [P, HALF], scope=s3)
        m = sb("m", [P, KT, S])
        with ExitStack() as s4:
            x2 = sb("x2", [P, TT, D], scope=s4)
        acc = sb("acc", [P, KT, S])
        relu = [sb(f"relu{s}", [P, HALF]) for s in range(2)]
        fsq = [sb(f"fsq{s}", [P, HALF]) for s in range(2)]
        ssq = [sb(f"ssq{s}", [P, HALF]) for s in range(2)]
        dev = sb("dev", [P, HALF])
        rstd = sb("rstd", [P, HALF])
        with ExitStack() as s5:
            f_hl = [sb("f_hi", [P, FFC, S], F32R, s5), sb("f_lo", [P, FFC, S], F32R, s5)]
        ost = [sb(f"ost{s}", [P, D]) for s in range(2)]

        psum = ctx.enter_context(nc.psum_tensor("psum", [P, 8, HALF], F32))
        SB, TBK = 2, 6
        gates = nc.dram_tensor("gates_scratch", [2, KT, P, S], F32, kind="Internal").ap()

        x_landed = [sem(f"x_landed{t}") for t in range(TT)]
        par_landed = sem("par_landed")
        setup = sem("setup")
        vec_setup = sem("vector_setup")
        par_t = sem("par_transposed")
        par_ready = sem("par_ready")
        dots_ready = sem("lambda_dots_ready")
        dot_exp_ready = sem("lambda_exp_ready")
        row_sums = sem("row_sums")
        row_dev = sem("row_deviations")
        row_rstd = sem("row_rstd")
        xn_ready = sem("x_normed")
        xt_done = sem("x_transposed")
        u_hi = sem("u_hi")
        u_ready = sem("u_ready")
        w_landed = [sem(f"w_landed{s}") for s in range(RING)]
        w_hi = sem("w_hi_ready")
        w_split = sem("w_split")
        proj_done = sem("proj_done")
        qk_hi = sem("qk_hi")
        qk_ready = sem("qk_ready")
        vt_ready = sem("vt_ready")
        h_ready = sem("h_ready")
        c_ready = sem("c_times_h_ready")
        taps = sem("conv_taps")
        z_ready = sem("z_ready")
        bias_ready = sem("gate_bias_ready")
        gate_ready = sem("gate_ready")
        gate_stored = [sem(f"gate_stored{s}") for s in range(2)]
        tb_done = sem("tb_done")
        tb_hi = sem("tb_hi")
        tb_free = sem("tb_free")
        s_done = sem("scores_done")
        s_read = sem("scores_read")
        table_ready = sem("alibi_scaled")
        max_ready = sem("max_ready")
        exp_done = sem("exp_done")
        combine = sem("combine_steps")
        a_ready = sem("a_ready")
        zhi_ready = sem("z_hi_ready")
        zlo_ready = sem("z_lo_ready")
        osq_ready = sem("o_squares_ready")
        osum_done = sem("o_sums_done")
        odev_ready = sem("o_deviations_ready")
        orstd_ready = sem("o_rstd_ready")
        o_scaled = sem("o_scaled")
        ohi_ready = sem("o_hi_ready")
        olo_ready = sem("o_lo_ready")
        gate_landed = [sem(f"gate_landed{s}") for s in range(2)]
        br_done = sem("branches_done")
        br_read = sem("branches_read")
        merge_steps = sem("merge_steps")
        merged_ready = sem("merged_ready")
        wo_done = sem("wo_done")
        m_ready = sem("m_ready")
        msq_ready = sem("m_squares_ready")
        msq_added = sem("m_squares_added")
        x2_landed = sem("x2_landed")
        msum_done = sem("m_sums_done")
        dev_ready = sem("deviations_ready")
        rstd_ready = sem("rstd_ready")
        res_done = sem("residual_transposed")
        m_scaled = sem("m_scaled")
        h_sum_ready = sem("residual_added")
        sq_ready = sem("squares_ready")
        sq_summed = sem("squares_summed")
        u2_scaled = sem("u2_scaled")
        u2_hi = sem("u2_hi")
        u2_ready = sem("u2_ready")
        ff_done = sem("ff_done")
        relu_done = sem("relu_done")
        fsq_ready = sem("relu_squared")
        fhi_ready = sem("f_hi_ready")
        f_ready = sem("f_ready")
        acc_done = sem("acc_done")
        y_scaled = sem("y_scaled")
        y_ready = sem("y_ready")
        yt_done = sem("y_transposed")
        ost_ready = [sem(f"ost_ready{s}") for s in range(2)]
        stored = [sem(f"stored{s}") for s in range(2)]

        x_tiles = x.rearrange("b (t p) d -> p (b t) d", p=P)
        out_tiles = out.rearrange("b (t p) d -> p (b t) d", p=P)
        w_in_t, w_co_t, w_ao_t, w_o_t, w1_t, w2_t = (
            w.rearrange("l (k p) n -> p (l k) n", p=P) for w in (w_in, w_conv_out, w_attn_out, w_o, w_ff1, w_ff2))

        P_BR = HEADS * HEAD_PANELS
        P_WO = P_BR + KT
        P_FF = P_WO + KT
        FF_PANELS = FFC + KT // 2
        P_END = P_FF + CHUNKS * FF_PANELS
        O_UNITS = HEADS * NH
        FF1_UNITS, FF2_UNITS = NH * FFC, NH * KT
        FF_UNITS = FF1_UNITS + FF2_UNITS
        tb_tiles = psum[:, TBK:TBK + 2].rearrange("p b (k c) -> p (b k) c", c=P)
        half_cols = [slice(h * HALF, (h + 1) * HALF) for h in range(NH)]

        def wait(eng, semaphore, value):
            if not isinstance(value, int) or value > 0:
                eng.wait_ge(semaphore, value)

        block = ctx.enter_context(nc.Block())

        @block.sync
        def _(sp):
            for t in range(TT):
                sp.dma_start(xn[:, t], x_tiles[:, t]).then_inc(x_landed[t], 16)
                if t == 0:
                    for src, a, b in ((norm_g, PAR_G, PAR_B), (b_gate, PAR_B, PAR_C), (conv_w, PAR_C, PAR_S)):
                        sp.dma_start(par_rows[a:b, :], src.rearrange("l n (k c) -> (l n k) c", c=P)
                                     ).then_inc(par_landed, 16)
                    sp.dma_start(par_rows[PAR_S:NPAR, :], subln_g).then_inc(par_landed, 16)
                    sp.dma_start(lqk[:].rearrange("p n c -> p (n c)"),
                                 lambda_qk.rearrange("l n c -> l (n c)").to_broadcast([P, 4 * HD])
                                 ).then_inc(par_landed, 16)

            def load(panel, slot, *pairs):
                wait(sp, w_split, panel - (RING - 1))
                for dst, src in pairs:
                    sp.dma_start(dst, src).then_inc(w_landed[slot], 32 // len(pairs))

            def head_panels(i):
                columns = [(COL_Q, 1), (COL_K, 1), (COL_V, 1), (COL_H, 1), (COL_C, 1), (COL_B, 1)]
                columns += [(COL_G + g * P, 4) for g in range(4)]
                for j, (col, stride) in enumerate(columns):
                    load(i * HEAD_PANELS + j, j % RING,
                         (w_raw[j % RING][:], w_in_t.rearrange("p k (b c) -> p k b c", c=P)
                          [:, :, bass.ds(i * stride + col // P, 1)].rearrange("p k b c -> p k (b c)")))

            head_panels(0)
            with sp.Fori(1, HEADS) as i:
                head_panels(i)
            with sp.Fori(0, KT // RING) as i:
                for j in range(RING):
                    cols = bass.ds(i * (RING * P) + j * P, P)
                    load(i * RING + (P_BR + j), j, (w_raw[j][:, 0:CT], w_co_t[:, :, cols]),
                         (w_raw[j][:, CT:KT], w_ao_t[:, :, cols]))
                    for h in range(NH):
                        sp.wait_ge(br_read, i * (4 * RING) + 4 * j + 2 * h + 2)
                        sp.dma_start(gate_in[h][:], gates[:, bass.ds(i * RING + j, 1), :, half_cols[h]]
                                     .rearrange("b o p c -> p (b o) c")).then_inc(gate_landed[h], 16)
            with sp.Fori(0, KT // RING) as i:
                for j in range(RING):
                    load(i * RING + (P_WO + j), j, (w_raw[j][:], w_o_t[:, :, bass.ds(i * (RING * P) + j * P, P)]))
            sp.wait_ge(br_done, 4 * KT)
            for t in range(TT):
                sp.dma_start(x2[:, t], x_tiles[:, t]).then_inc(x2_landed, 16)
            with sp.Fori(0, CHUNKS) as i:
                for j in range(FFC):
                    load(i * FF_PANELS + (P_FF + j), j % RING,
                         (w_raw[j % RING][:], w1_t[:, :, bass.ds(i * (FFC * P) + j * P, P)]))
                for j in range(KT // 2):
                    slot = (FFC + j) % RING
                    load(i * FF_PANELS + (P_FF + FFC + j), slot,
                         (w_raw[slot][:].rearrange("p (k d) c -> p k (d c)", d=2),
                          w2_t[:, bass.ds(i * FFC, FFC), j * 2 * P:(j + 1) * 2 * P]))
            for t in range(TT):
                sp.wait_ge(ost_ready[t % 2], 2 * (t // 2 + 1))
                sp.dma_start(out_tiles[:, t], ost[t % 2][:]).then_inc(stored[t % 2], 16)
            for s in range(2):
                sp.wait_ge(stored[s], 16 * (TT // 2))

        @block.gpsimd
        def _(pool):
            nc.gpsimd.memset(ident[:], 1.0).then_inc(setup, 1)
            pool.wait_ge(setup, 1)
            nc.gpsimd.affine_select(out=ident[:], in_=ident[:], compare_op=ALU.is_equal, fill=0.0, base=0,
                                    pattern=[[-1, P]], channel_multiplier=1).then_inc(setup, 1)
            nc.gpsimd.memset(ones[:], 1.0).then_inc(setup, 1)
            nc.gpsimd.iota(table[:], [[-1, 2 * S - P]], base=S - P, channel_multiplier=1,
                           allow_small_or_imprecise_dtypes=True).then_inc(setup, 1)
            nc.gpsimd.memset(inner[:], 0.0).then_inc(setup, 1)
            pool.wait_ge(wo_done, 1)
            for h in range(NH):
                nc.gpsimd.memset(ssq[h][:], 0.0).then_inc(msq_added, 1)
            pool.wait_ge(msq_added, NH)
            with pool.Fori(0, KT) as i:
                for h in range(NH):
                    pool.wait_ge(msq_ready, i * NH + (h + 1))
                    pool.wait_ge(msq_added, i * NH + (h + NH - 1))
                    nc.gpsimd.tensor_tensor(ssq[h][:], ssq[h][:], fsq[h][:], ALU.add).then_inc(msq_added, 1)
            pool.wait_ge(res_done, NH * KT)
            nc.gpsimd.memset(acc[:], 0.0).then_inc(acc_done, FF2_UNITS)

        @block.tensor
        def _(pe):
            pe.sem_inc(m_ready, 2)
            pe.sem_inc(f_ready, 2)

            def product(bank, stat, moving, kts):
                terms = [(kt, a, b) for kt in kts for a, b in PASSES]
                for t, (kt, a, b) in enumerate(terms):
                    mm = nc.tensor.matmul(bank, stat(a, kt), moving(b, kt), start=(t == 0),
                                          stop=(t == len(terms) - 1))
                return mm

            pe.wait_ge(par_landed, 16 * 5)
            pe.wait_ge(setup, 5)
            nc.tensor.transpose(psum[:, 7, 0:NPAR], par_rows[:], ident[0:NPAR, 0:NPAR]).then_inc(par_t, 1)
            for h in range(NH):
                pe.wait_ge(xn_ready, (h + 1) * (TT // NH))
                for kt in range(KT):
                    n = h * KT + kt
                    wait(pe, u_ready, n - 3)
                    for t in range(4):
                        mm = nc.tensor.transpose(psum[:, n % 4, t * P:(t + 1) * P],
                                                 xn[:, 4 * h + t, kt * P:(kt + 1) * P], ident[:])
                    mm.then_inc(xt_done, 1)
            pe.wait_ge(u_ready, NH * KT)

            def walk(i, steps):
                for kind, n in steps:
                    if kind in PANELS:
                        u = unit_of(kind, n)
                        j, h = u // 2, u % 2
                        slot = j % RING
                        if h == 0:
                            pe.wait_ge(w_split, i * HEAD_PANELS + (j + 1))
                        if kind == "q":
                            wait(pe, gate_ready, i * 8 - (1 - h))
                        elif kind == "k":
                            pe.wait_ge(qk_ready, i * 4 + (1 + h))
                        elif kind == "v":
                            pe.wait_ge(qk_ready, i * 4 + (3 + h))
                        elif kind == "h":
                            pe.wait_ge(vt_ready, i * 2 + (1 + h))
                        elif kind == "c":
                            pe.wait_ge(h_ready, i * 2 + (1 + h))
                        elif kind == "b":
                            pe.wait_ge(c_ready, i * 2 + (1 + h))
                        elif n < 2:
                            pe.wait_ge(z_ready, i * 2 + (1 + h))
                        else:
                            pe.wait_ge(gate_ready, i * 8 + (n - 1))
                        product(psum[:, h], lambda a, kt: w_hl[slot][a][:, kt],
                                lambda b, kt: act_hl[b][:, kt, half_cols[h]], range(KT)).then_inc(proj_done, 1)
                    elif kind == "S":
                        if n == 0:
                            pe.wait_ge(qk_ready, i * 4 + 4)
                        wait(pe, s_read, i * QB + n)
                        for a, b in PASSES:
                            for half in range(NH):
                                for c in range(2):
                                    rows = slice(c * HD, (c + 1) * HD)
                                    mm = nc.tensor.matmul(psum[:, SB + 2 * c + half],
                                                          q_hl[a][rows, n * P:(n + 1) * P],
                                                          k_hl[b][rows, half_cols[half]],
                                                          start=((a, b) == PASSES[0]), stop=((a, b) == PASSES[-1]))
                        mm.then_inc(s_done, 1)
                    elif kind in ("VT", "T"):
                        if kind == "VT":
                            pe.wait_ge(vt_ready, i * 2 + 2)
                        else:
                            pe.wait_ge(a_ready, i * QB + (n + 1 if n < 7 else 0))
                        wait(pe, tb_free, tb_use(i, kind, n))
                        src = vt if kind == "VT" else e[0]
                        for k in range(TT):
                            mm = nc.tensor.transpose(psum[:, TBK + k // 4, (k % 4) * P:(k % 4 + 1) * P],
                                                     src[:, k * P:(k + 1) * P], ident[:])
                        mm.then_inc(tb_done, 1)
                    elif kind == "AV":
                        pe.wait_ge(tb_free, tb_use(i, kind, n))
                        product(psum[:, TBK], lambda a, kt: v_hl[a][:, kt], lambda b, kt: at_hl[b][:, kt],
                                range(TT)).then_inc(tb_done, 1)

            walk(0, OPENING + REST)
            with pe.Fori(1, HEADS) as i:
                walk(i, OPENING_WITH_TAIL + REST)
            walk(HEADS, TAIL)

            for s in range(2):
                pe.wait_ge(gate_stored[s], 16 * 4 * HEADS)
            pe.wait_ge(tb_free, HEADS * TB_USES)
            pe.sem_inc(br_read, 4)
            for n in range(O_UNITS):
                pe.wait_ge(osq_ready, n + 1)
                wait(pe, odev_ready, n - 1)
                nc.tensor.matmul(psum[:, TBK + n % 2], ones[:], osq[n % 2][:], start=True, stop=True
                                 ).then_inc(osum_done, 1)

            pe.wait_ge(gate_ready, 8 * HEADS)
            pe.wait_ge(zlo_ready, CT)
            pe.wait_ge(olo_ready, O_UNITS)
            with pe.Fori(0, KT // RING) as i:
                for j in range(RING):
                    pe.wait_ge(w_split, i * RING + (P_BR + j + 1))
                    for h in range(NH):
                        for br in range(2):
                            pe.wait_ge(br_read, i * (4 * RING) + (4 * j + 2 * h + br + 1))
                            src = (z_hl, o_hl)[br]
                            product(psum[:, 2 * h + br], lambda a, kt: w_hl[j][a][:, CT * br + kt],
                                    lambda b, kt: src[b][:, kt, half_cols[h]], range(CT)).then_inc(br_done, 1)

            pe.wait_ge(br_read, 4 * KT + 4)
            pe.wait_ge(merged_ready, NH * KT)
            with pe.Fori(0, KT // RING) as i:
                for j in range(RING):
                    pe.wait_ge(w_split, i * RING + (P_WO + j + 1))
                    for h in range(NH):
                        pe.wait_ge(m_ready, i * (RING * NH) + (NH * j + h + 1))
                        product(psum[:, h], lambda a, kt: w_hl[j][a][:, kt],
                                lambda b, kt: act_hl[b][:, kt, half_cols[h]], range(KT)).then_inc(wo_done, 1)

            pe.wait_ge(x2_landed, 16 * TT)
            pe.wait_ge(msq_added, NH + NH * KT)
            pe.wait_ge(m_ready, NH * KT + 2)
            for h in range(NH):
                nc.tensor.matmul(psum[:, 4], ones[:], ssq[h][:], start=True, stop=True).then_inc(msum_done, 1)
                for kt in range(KT):
                    n = h * KT + kt
                    wait(pe, h_sum_ready, n - 3)
                    for t in range(4):
                        mm = nc.tensor.transpose(psum[:, n % 4, t * P:(t + 1) * P],
                                                 x2[:, 4 * h + t, kt * P:(kt + 1) * P], ident[:])
                    mm.then_inc(res_done, 1)
                for kt in range(KT):
                    n = h * KT + kt
                    pe.wait_ge(sq_ready, n + 1)
                    nc.tensor.matmul(psum[:, 5], ones[:], fsq[n % 2][:], start=(kt == 0), stop=(kt == KT - 1)
                                     ).then_inc(sq_summed, 1)
                pe.wait_ge(dev_ready, 2 * h + 2)

            pe.wait_ge(h_sum_ready, NH * KT)
            pe.wait_ge(u2_ready, NH * KT)
            with pe.Fori(0, CHUNKS) as i:
                for j in range(FFC):
                    pe.wait_ge(w_split, i * FF_PANELS + (P_FF + j + 1))
                    for h in range(NH):
                        u = NH * j + h
                        if u < 4:
                            pe.wait_ge(acc_done, i * FF2_UNITS + (FF2_UNITS - 3 + u))
                        else:
                            pe.wait_ge(relu_done, i * FF1_UNITS + (u - 3))
                        product(psum[:, u % 4], lambda a, kt: w_hl[j % RING][a][:, kt],
                                lambda b, kt: act_hl[b][:, kt, half_cols[h]], range(KT)).then_inc(ff_done, 1)
                for j in range(KT // 2):
                    slot = (FFC + j) % RING
                    pe.wait_ge(w_split, i * FF_PANELS + (P_FF + FFC + j + 1))
                    for dd in range(2):
                        for h in range(NH):
                            u = 4 * j + 2 * dd + h
                            if u < NH:
                                pe.wait_ge(f_ready, i * FF1_UNITS + (2 + FF1_UNITS - 1 + h))
                            if u < 4:
                                pe.wait_ge(relu_done, i * FF1_UNITS + (FF1_UNITS - 3 + u))
                            else:
                                pe.wait_ge(acc_done, i * FF2_UNITS + (FF2_UNITS + u - 3))
                            product(psum[:, u % 4], lambda a, kt: w_hl[slot][a][:, 2 * kt + dd],
                                    lambda b, kt: f_hl[b][:, kt, half_cols[h]], range(FFC)).then_inc(ff_done, 1)

            for h in range(NH):
                for kt in range(KT):
                    n = (NH + h) * KT + kt
                    pe.wait_ge(sq_ready, n + 1)
                    nc.tensor.matmul(psum[:, 6 + h], ones[:], fsq[n % 2][:], start=(kt == 0), stop=(kt == KT - 1)
                                     ).then_inc(sq_summed, 1)
            pe.wait_ge(acc_done, (CHUNKS + 1) * FF2_UNITS)
            for t in range(TT):
                if t % 4 == 0:
                    pe.wait_ge(y_ready, KT * (t // 4 + 1))
                wait(pe, ost_ready[t % 2], 2 * (t // 2))
                for kt in range(KT):
                    mm = nc.tensor.transpose(psum[:, 2 * (t % 2) + kt // 4, (kt % 4) * P:(kt % 4 + 1) * P],
                                             m[:, kt, t * P:(t + 1) * P], ident[:])
                mm.then_inc(yt_done, 1)

        @block.scalar
        def _(act):
            def split_hi(panel, slot, turns):
                act.wait_ge(w_landed[slot], turns * 32 + 32)
                nc.scalar.activation(w_hl[slot][0][:], w_raw[slot][:], ACT.Copy).then_inc(w_hi, 1)

            def squares(n, src):
                wait(act, sq_summed, n - 1)
                nc.scalar.activation(fsq[n % 2][:], src, ACT.Square).then_inc(sq_ready, 1)

            act.wait_ge(dots_ready, 2)
            nc.scalar.activation(dot_exp, dots, ACT.Exp).then_inc(dot_exp_ready, 1)
            act.wait_ge(vec_setup, 1)
            for h in range(NH):
                for t in range(4 * h, 4 * h + 4):
                    act.wait_ge(x_landed[t], 16)
                    wait(act, row_sums, t)
                    nc.scalar.activation(xsq[:], xn[:, t], ACT.Square, accum_out=stats[:, t:t + 1]
                                         ).then_inc(row_sums, 1)
                act.wait_ge(row_sums, 4 * h + 4)
                nc.scalar.activation(stats[:, TT + 4 * h:TT + 4 * h + 4], stats[:, 4 * h:4 * h + 4], ACT.Sqrt,
                                     bias=eps, scale=1.0 / D).then_inc(row_dev, 1)
            act.wait_ge(par_ready, 1)
            for h in range(NH):
                for kt in range(KT):
                    n = h * KT + kt
                    act.wait_ge(xt_done, n + 1)
                    nc.scalar.activation(act_hl[0][:, kt, half_cols[h]], psum[:, n % 4], ACT.Copy,
                                         scale=par[:, PAR_G + kt:PAR_G + kt + 1]).then_inc(u_hi, 1)
            nc.scalar.preload_act_table(ACT.Exp)
            split_hi(0, 0, 0)

            def walk(i, steps):
                for kind, n in steps:
                    if kind in PANELS:
                        u = unit_of(kind, n)
                        j, h = u // 2, u % 2
                        if kind not in "cb" or h == 0:
                            act.wait_ge(proj_done, i * HEAD_UNITS + (u + 1))
                        if kind in "qk":
                            nc.scalar.activation((q_hl if kind == "q" else k_hl)[0][:, half_cols[h]], psum[:, h],
                                                 ACT.Copy).then_inc(qk_hi, 1)
                        elif kind == "v":
                            nc.scalar.activation(vt[:, half_cols[h]], psum[:, h], ACT.Copy).then_inc(vt_ready, 1)
                        elif kind == "h":
                            nc.scalar.activation(inner[:, 1 + h * HALF:1 + (h + 1) * HALF], psum[:, h], ACT.Copy
                                                 ).then_inc(h_ready, 1)
                        elif kind == "g":
                            if n == 0:
                                act.wait_ge(bias_ready, i + 1)
                            wait(act, gate_stored[h], i * 64 + 16 * (n // 2))
                            nc.scalar.activation(gate_out[h][:], psum[:, h], ACT.Tanh, scale=0.5,
                                                 bias=gate_bias[:, n // 2:n // 2 + 1]).then_inc(gate_ready, 1)
                            act.wait_ge(gate_ready, i * 8 + (n + 1))
                            act.dma_start(one(gates.rearrange("b k p s -> p (b k) s"), i * 4 + n // 2)[:, half_cols[h]],
                                          gate_out[h][:]).then_inc(gate_stored[h], 16)
                        if h == 0:
                            split_hi(i * HEAD_PANELS + (j + 1), (j + 1) % RING,
                                     i * (HEAD_PANELS // RING) + (j + 1) // RING)
                    elif kind == "M":
                        act.wait_ge(max_ready, i * QB + (n + 1))
                        for c in range(2):
                            nc.scalar.activation(e[c][:], e[c][:], ACT.Exp, scale=SCALE, bias=neg_max[:, c:c + 1],
                                                 accum_out=exp_sum[:, c:c + 1]).then_inc(exp_done, 1)
                    elif kind in ("VT", "T"):
                        act.wait_ge(tb_done, tb_use(i, kind, n) + 1)
                        dst = v_hl[0][:] if kind == "VT" else at_hl[0][:, :, (n % 4) * P:(n % 4 + 1) * P]
                        nc.scalar.activation(dst, tb_tiles, ACT.Copy).then_inc(tb_hi, 1)

            walk(0, OPENING + REST)
            with act.Fori(1, HEADS) as i:
                walk(i, OPENING_WITH_TAIL + REST)
            walk(HEADS, TAIL)

            act.wait_ge(tb_free, HEADS * TB_USES)
            for s in range(2):
                act.wait_ge(gate_stored[s], 16 * 4 * HEADS)
            for ct in range(CT):
                nc.scalar.activation(z_hl[0][:, ct], z[:, ct], ACT.Copy).then_inc(zhi_ready, 1)
            nc.scalar.preload_act_table(ACT.Sqrt)

            def o_square(n):
                wait(act, osum_done, n - 1)
                nc.scalar.activation(osq[n % 2][:], o[:, n // NH, half_cols[n % NH]], ACT.Square
                                     ).then_inc(osq_ready, 1)

            o_square(0)
            for n in range(O_UNITS):
                if n + 1 < O_UNITS:
                    o_square(n + 1)
                act.wait_ge(osum_done, n + 1)
                wait(act, orstd_ready, n)
                nc.scalar.activation(odev[:], psum[:, TBK + n % 2], ACT.Sqrt, bias=eps, scale=1.0 / (2 * HD)
                                     ).then_inc(odev_ready, 1)
                act.wait_ge(o_scaled, n + 1)
                nc.scalar.activation(o_hl[0][:, n // NH, half_cols[n % NH]], o[:, n // NH, half_cols[n % NH]],
                                     ACT.Copy).then_inc(ohi_ready, 1)

            with act.Fori(0, KT // RING) as i:
                for j in range(RING):
                    act.wait_ge(br_done, i * (4 * RING) + (4 * j + 1))
                    split_hi(i * RING + (P_BR + j + 1), (j + 1) % RING, i + (P_BR + j + 1) // RING)
            with act.Fori(0, KT // RING) as i:
                for j in range(RING):
                    for h in range(NH):
                        n = NH * j + h
                        act.wait_ge(wo_done, i * (RING * NH) + (n + 1))
                        act.wait_ge(msq_added, i * (RING * NH) + (n + 1))
                        nc.scalar.activation(fsq[h][:], psum[:, h], ACT.Square).then_inc(msq_ready, 1)
                        if h == 0:
                            split_hi(i * RING + (P_WO + j + 1), (j + 1) % RING, i + (P_WO + j + 1) // RING)

            act.wait_ge(msq_added, NH + NH * KT)
            for h in range(NH):
                act.wait_ge(msum_done, h + 1)
                wait(act, rstd_ready, 2 * h)
                nc.scalar.activation(dev[:], psum[:, 4], ACT.Sqrt, bias=eps, scale=1.0 / D).then_inc(dev_ready, 1)
                for kt in range(KT):
                    n = h * KT + kt
                    act.wait_ge(h_sum_ready, n + 1)
                    squares(n, m[:, kt, half_cols[h]])
                act.wait_ge(sq_summed, (h + 1) * KT)
                act.wait_ge(rstd_ready, 2 * h + 1)
                nc.scalar.activation(dev[:], psum[:, 5], ACT.Sqrt, bias=eps, scale=1.0 / D).then_inc(dev_ready, 1)
                for kt in range(KT):
                    n = h * KT + kt
                    act.wait_ge(u2_scaled, n + 1)
                    nc.scalar.activation(act_hl[0][:, kt, half_cols[h]], relu[n % 2][:], ACT.Copy
                                         ).then_inc(u2_hi, 1)

            def chunk(i, last):
                for j in range(FF_PANELS):
                    if j < FFC:
                        for h in range(NH):
                            u = NH * j + h
                            act.wait_ge(ff_done, i * FF_UNITS + (u + 1))
                            nc.scalar.activation(relu[h][:], psum[:, u % 4], ACT.Relu).then_inc(relu_done, 1)
                            if h == 0:
                                split_hi(i * FF_PANELS + (P_FF + j + 1), (j + 1) % RING,
                                         i * (FF_PANELS // RING) + (P_FF + j + 1) // RING)
                            act.wait_ge(relu_done, i * FF1_UNITS + (u + 1))
                            act.wait_ge(f_ready, i * FF1_UNITS + (u + 1))
                            nc.scalar.activation(fsq[h][:], relu[h][:], ACT.Square).then_inc(fsq_ready, 1)
                    elif not (last and j == FF_PANELS - 1):
                        act.wait_ge(ff_done, i * FF_UNITS + (FF1_UNITS + 4 * (j - FFC) + 1))
                        split_hi(i * FF_PANELS + (P_FF + j + 1), (j + 1) % RING,
                                 i * (FF_PANELS // RING) + (P_FF + j + 1) // RING)

            with act.Fori(0, CHUNKS - 1) as i:
                chunk(i, False)
            chunk(CHUNKS - 1, True)

            act.wait_ge(acc_done, (CHUNKS + 1) * FF2_UNITS)
            act.wait_ge(f_ready, 2 + CHUNKS * FF1_UNITS)
            for h in range(NH):
                for kt in range(KT):
                    squares((NH + h) * KT + kt, acc[:, kt, half_cols[h]])
                act.wait_ge(sq_summed, (NH + h + 1) * KT)
                act.wait_ge(rstd_ready, 2 * NH + h)
                nc.scalar.activation(dev[:], psum[:, 6 + h], ACT.Sqrt, bias=eps, scale=1.0 / D
                                     ).then_inc(dev_ready, 1)
            for t in range(TT):
                act.wait_ge(yt_done, t + 1)
                wait(act, stored[t % 2], 16 * (t // 2))
                nc.scalar.activation(ost[t % 2][:, 0:HALF], psum[:, 2 * (t % 2)], ACT.Copy
                                     ).then_inc(ost_ready[t % 2], 1)

        @block.vector
        def _(dve):
            vec = nc.vector

            def lo_part(dst_hl, idx, src, semaphore, gain=None):
                hi, lo = dst_hl[0][idx].bitcast(F32), dst_hl[1][idx]
                if gain is None:
                    return vec.tensor_tensor(lo, src, hi, ALU.subtract).then_inc(semaphore, 1)
                return vec.scalar_tensor_tensor(out=lo, in0=src, scalar=gain, in1=hi, op0=ALU.mult,
                                                op1=ALU.subtract).then_inc(semaphore, 1)

            def split_lo(panel, slot):
                dve.wait_ge(w_hi, panel + 1)
                vec.tensor_tensor(w_hl[slot][1][:], w_raw[slot][:], w_hl[slot][0][:].bitcast(F32), ALU.subtract
                                  ).then_inc(w_split, 1)

            vec.memset(eps, EPS).then_inc(vec_setup, 1)
            dve.wait_ge(par_landed, 16 * 5)
            for c in range(2):
                wait(dve, dots_ready, c)
                vec.tensor_tensor_reduce(out=lq_junk[:], in0=lqk[:, 2 * c], in1=lqk[:, 2 * c + 1], scale=1.0,
                                         scalar=0.0, op0=ALU.mult, op1=ALU.add, accum_out=dots[:, c:c + 1]
                                         ).then_inc(dots_ready, 1)
            dve.wait_ge(par_t, 1)
            vec.tensor_copy(par[:, 0:NPAR], psum[:, 7, 0:NPAR]).then_inc(par_ready, 1)
            dve.wait_ge(par_ready, 1)
            vec.tensor_scalar(bhalf[:], par[:, PAR_B:PAR_C], 0.5, None, ALU.mult).then_inc(vec_setup, 1)
            vec.tensor_scalar(sub_gain, par[:, PAR_S:NPAR], 1.0 - LAM_INIT, None, ALU.mult).then_inc(vec_setup, 1)
            dve.wait_ge(dot_exp_ready, 1)
            vec.tensor_tensor(lam_diff, dot_exp[:, 1:2], dot_exp[:, 0:1], ALU.subtract).then_inc(vec_setup, 1)
            dve.wait_ge(vec_setup, 4)
            vec.tensor_scalar(neg_lam, lam_diff, -LAM_INIT, None, ALU.add).then_inc(vec_setup, 1)
            for h in range(NH):
                dve.wait_ge(row_dev, h + 1)
                cols = slice(TT + 4 * h, TT + 4 * h + 4)
                vec.reciprocal(stats[:, cols], stats[:, cols]).then_inc(row_rstd, 1)
                dve.wait_ge(row_rstd, h + 1)
                for t in range(4 * h, 4 * h + 4):
                    vec.tensor_scalar(xn[:, t], xn[:, t], stats[:, TT + t:TT + t + 1], None, ALU.mult
                                      ).then_inc(xn_ready, 1)
            dve.wait_ge(setup, 5)
            vec.scalar_tensor_tensor(out=table[:], in0=table[:], scalar=-1.0, in1=table[:], op0=ALU.mult,
                                     op1=ALU.min).then_inc(vec_setup, 1)
            dve.wait_ge(vec_setup, 6)
            vec.tensor_scalar(table[:], table[:], SLOPES[0] / SCALE, None, ALU.mult).then_inc(table_ready, 1)
            for h in range(NH):
                for kt in range(KT):
                    n = h * KT + kt
                    dve.wait_ge(u_hi, n + 1)
                    lo_part(act_hl, (slice(None), kt, half_cols[h]), psum[:, n % 4], u_ready,
                            par[:, PAR_G + kt:PAR_G + kt + 1])
            split_lo(0, 0)

            def walk(i, steps):
                for kind, n in steps:
                    if kind in PANELS:
                        u = unit_of(kind, n)
                        j, h = u // 2, u % 2
                        cols = half_cols[h]
                        if kind in "qk":
                            dve.wait_ge(qk_hi, i * 4 + (u + 1))
                            lo_part(q_hl if kind == "q" else k_hl, (slice(None), cols), psum[:, h], qk_ready)
                        elif kind == "c":
                            dve.wait_ge(proj_done, i * HEAD_UNITS + (u + 1))
                            dve.wait_ge(h_ready, i * 2 + (h + 1))
                            span = inner[:, 1 + h * HALF:1 + (h + 1) * HALF]
                            vec.tensor_tensor(span, psum[:, h], span, ALU.mult).then_inc(c_ready, 1)
                            if h == 0:
                                vec.tensor_copy(gate_bias[:], bhalf[:, bass.ds(i * 4, 4)]).then_inc(bias_ready, 1)
                            else:
                                for tap in range(CONV_K):
                                    wc = par[:, bass.ds(i + (PAR_C + tap * CT), 1)]
                                    win = inner[:, tap:tap + S]
                                    if tap == 0:
                                        dve.wait_ge(c_ready, i * 2 + 2)
                                        vec.tensor_scalar(one(z, i), win, wc, None, ALU.mult).then_inc(taps, 1)
                                    else:
                                        dve.wait_ge(taps, i * CONV_K + tap)
                                        vec.scalar_tensor_tensor(out=one(z, i), in0=win, scalar=wc, in1=one(z, i),
                                                                 op0=ALU.mult, op1=ALU.add).then_inc(taps, 1)
                        elif kind == "b":
                            dve.wait_ge(proj_done, i * HEAD_UNITS + (u + 1))
                            dve.wait_ge(taps, i * CONV_K + CONV_K)
                            vec.tensor_tensor(one(z, i)[:, cols], psum[:, h], one(z, i)[:, cols], ALU.mult
                                              ).then_inc(z_ready, 1)
                        if h == 0:
                            split_lo(i * HEAD_PANELS + (j + 1), (j + 1) % RING)
                    elif kind == "M":
                        if n == 0 and not isinstance(i, int):
                            vec.tensor_scalar(table[:], table[:], SLOPES[1] / SLOPES[0], None, ALU.mult
                                              ).then_inc(table_ready, 1)
                        if n == 0:
                            dve.wait_ge(table_ready, i + 1)
                        dve.wait_ge(s_done, i * QB + (n + 1))
                        vec.memset(spare, 0.0)
                        start = S - P - P * n
                        for c in range(2):
                            ins = vec.tensor_tensor_reduce(
                                out=e[c][:], in0=psum[:, SB + 2 * c:SB + 2 * c + 2].rearrange("p b c -> p (b c)"),
                                in1=table[:, start:start + S], scale=1.0, scalar=-3.0e38, op0=ALU.add, op1=ALU.max,
                                accum_out=maxima[:, c:c + 1])
                        ins.then_inc(s_read, 1)
                        dve.wait_ge(s_read, i * QB + (n + 1))
                        vec.tensor_scalar(neg_max, maxima, -SCALE, None, ALU.mult).then_inc(max_ready, 1)
                    elif kind == "C":
                        blk = i * QB + (n if n < 7 else -1)
                        dve.wait_ge(exp_done, blk * 2 + 2)
                        vec.reciprocal(recip, exp_sum).then_inc(combine, 1)
                        dve.wait_ge(combine, blk * 3 + 1)
                        vec.tensor_scalar(weight2, recip[:, 1:2], neg_lam, None, ALU.mult).then_inc(combine, 1)
                        dve.wait_ge(combine, blk * 3 + 2)
                        vec.tensor_scalar(e[1][:], e[1][:], weight2, None, ALU.mult).then_inc(combine, 1)
                        dve.wait_ge(combine, blk * 3 + 3)
                        vec.scalar_tensor_tensor(out=e[0][:], in0=e[0][:], scalar=recip[:, 0:1], in1=e[1][:],
                                                 op0=ALU.mult, op1=ALU.add).then_inc(a_ready, 1)
                    elif kind in ("VT", "T"):
                        dve.wait_ge(tb_hi, i * (QB + 1) + {"VT": 1, "T": 2 + n if n < 7 else 0}[kind])
                        if kind == "VT":
                            lo_part(v_hl, slice(None), tb_tiles, tb_free)
                        else:
                            lo_part(at_hl, (slice(None), slice(None), slice((n % 4) * P, (n % 4 + 1) * P)), tb_tiles,
                                    tb_free)
                    elif kind == "AV":
                        dve.wait_ge(tb_done, tb_use(i, kind, n) + 1)
                        vec.tensor_scalar(one(o, i - n)[:, half_cols[n]], psum[:, TBK], 1.0, None, ALU.mult
                                          ).then_inc(tb_free, 1)

            walk(0, OPENING + REST)
            with dve.Fori(1, HEADS) as i:
                walk(i, OPENING_WITH_TAIL + REST)
            walk(HEADS, TAIL)

            for ct in range(CT):
                dve.wait_ge(zhi_ready, ct + 1)
                lo_part(z_hl, (slice(None), ct), z[:, ct], zlo_ready)
            for n in range(O_UNITS):
                span = o[:, n // NH, half_cols[n % NH]]
                dve.wait_ge(odev_ready, n + 1)
                vec.reciprocal(prod[0][:], odev[:]).then_inc(orstd_ready, 1)
                dve.wait_ge(orstd_ready, n + 1)
                vec.scalar_tensor_tensor(out=span, in0=span, scalar=sub_gain, in1=prod[0][:], op0=ALU.mult,
                                         op1=ALU.mult).then_inc(o_scaled, 1)
                dve.wait_ge(ohi_ready, n + 1)
                lo_part(o_hl, (slice(None), n // NH, half_cols[n % NH]), span, olo_ready)

            with dve.Fori(0, KT // RING) as i:
                for j in range(RING):
                    for h in range(NH):
                        n = NH * j + h
                        for br in range(2):
                            if br == 0:
                                dve.wait_ge(gate_landed[h], i * (16 * RING) + 16 * (j + 1))
                            dve.wait_ge(br_done, i * (4 * RING) + (2 * n + br + 1))
                            vec.scalar_tensor_tensor(out=prod[br][:], in0=gate_in[h][:, br], scalar=1.0,
                                                     in1=psum[:, 2 * h + br], op0=ALU.add, op1=ALU.mult
                                                     ).then_inc(br_read, 1)
                            if br == 0 and h == 0:
                                split_lo(i * RING + (P_BR + j + 1), (j + 1) % RING)
                        dve.wait_ge(br_read, i * (4 * RING) + (4 + 2 * n + 2))
                        vec.tensor_tensor(prod[2][:], prod[0][:], prod[1][:], ALU.add).then_inc(merge_steps, 1)
                        hi = one(act_hl[0], i * RING + j)[:, half_cols[h]]
                        lo = one(act_hl[1], i * RING + j)[:, half_cols[h]]
                        dve.wait_ge(merge_steps, i * (4 * RING) + (2 * n + 1))
                        vec.tensor_scalar(hi, prod[2][:], 0.5, None, ALU.mult).then_inc(merge_steps, 1)
                        dve.wait_ge(merge_steps, i * (4 * RING) + (2 * n + 2))
                        vec.scalar_tensor_tensor(out=lo, in0=prod[2][:], scalar=0.5, in1=hi.bitcast(F32),
                                                 op0=ALU.mult, op1=ALU.subtract).then_inc(merged_ready, 1)
            with dve.Fori(0, KT // RING) as i:
                for j in range(RING):
                    for h in range(NH):
                        dve.wait_ge(msq_ready, i * (RING * NH) + (NH * j + h + 1))
                        vec.tensor_scalar(one(m, i * RING + j)[:, half_cols[h]], psum[:, h], 1.0, None, ALU.mult
                                          ).then_inc(m_ready, 1)
                        if h == 0:
                            split_lo(i * RING + (P_WO + j + 1), (j + 1) % RING)

            def inverse(n):
                dve.wait_ge(dev_ready, n + 1)
                vec.reciprocal(rstd[:], dev[:]).then_inc(rstd_ready, 1)
                dve.wait_ge(rstd_ready, n + 1)

            def scale_by(out_ap, in_ap, norm, kt, semaphore):
                col = PAR_G + norm * KT + kt
                vec.scalar_tensor_tensor(out=out_ap, in0=in_ap, scalar=par[:, col:col + 1], in1=rstd[:],
                                         op0=ALU.mult, op1=ALU.mult).then_inc(semaphore, 1)

            for h in range(NH):
                inverse(2 * h)
                if h == 0:
                    dve.wait_ge(m_ready, NH * KT + 2)
                for kt in range(KT):
                    scale_by(m[:, kt, half_cols[h]], m[:, kt, half_cols[h]], 1, kt, m_scaled)
                for kt in range(KT):
                    n = h * KT + kt
                    span = m[:, kt, half_cols[h]]
                    dve.wait_ge(m_scaled, n + 1)
                    dve.wait_ge(res_done, n + 1)
                    vec.tensor_tensor(span, psum[:, n % 4], span, ALU.add).then_inc(h_sum_ready, 1)
                inverse(2 * h + 1)
                dve.wait_ge(h_sum_ready, (h + 1) * KT)
                for kt in range(KT + 1):
                    n = h * KT + kt
                    if kt < KT:
                        wait(dve, u2_ready, n - 1)
                        scale_by(relu[n % 2][:], m[:, kt, half_cols[h]], 2, kt, u2_scaled)
                    if kt > 0:
                        dve.wait_ge(u2_hi, n)
                        lo_part(act_hl, (slice(None), kt - 1, half_cols[h]), relu[(n - 1) % 2][:], u2_ready)

            def chunk(i, last):
                for j in range(FF_PANELS):
                    if j < FFC:
                        for h in range(NH):
                            u = NH * j + h
                            if h == 0:
                                split_lo(i * FF_PANELS + (P_FF + j + 1), (j + 1) % RING)
                            dve.wait_ge(fsq_ready, i * FF1_UNITS + (u + 1))
                            vec.tensor_copy(f_hl[0][:, j, half_cols[h]], fsq[h][:]).then_inc(fhi_ready, 1)
                            dve.wait_ge(fhi_ready, i * FF1_UNITS + (u + 1))
                            lo_part(f_hl, (slice(None), j, half_cols[h]), fsq[h][:], f_ready)
                    else:
                        for dd in range(2):
                            for h in range(NH):
                                u = 4 * (j - FFC) + 2 * dd + h
                                dve.wait_ge(ff_done, i * FF_UNITS + (FF1_UNITS + u + 1))
                                dve.wait_ge(acc_done, i * FF2_UNITS + (u + 1))
                                span = acc[:, 2 * (j - FFC) + dd, half_cols[h]]
                                vec.tensor_tensor(span, psum[:, u % 4], span, ALU.add).then_inc(acc_done, 1)
                                if dd == 0 and h == 0 and not (last and j == FF_PANELS - 1):
                                    split_lo(i * FF_PANELS + (P_FF + j + 1), (j + 1) % RING)

            dve.wait_ge(acc_done, FF2_UNITS)
            with dve.Fori(0, CHUNKS - 1) as i:
                chunk(i, False)
            chunk(CHUNKS - 1, True)

            for h in range(NH):
                inverse(2 * NH + h)
                for kt in range(KT):
                    scale_by(acc[:, kt, half_cols[h]], acc[:, kt, half_cols[h]], 3, kt, y_scaled)
                for kt in range(KT):
                    dve.wait_ge(y_scaled, h * KT + kt + 1)
                    vec.tensor_tensor(m[:, kt, half_cols[h]], m[:, kt, half_cols[h]], acc[:, kt, half_cols[h]],
                                      ALU.add).then_inc(y_ready, 1)
            for t in range(TT):
                dve.wait_ge(yt_done, t + 1)
                wait(dve, stored[t % 2], 16 * (t // 2))
                vec.tensor_copy(ost[t % 2][:, HALF:D], psum[:, 2 * (t % 2) + 1]).then_inc(ost_ready[t % 2], 1)


NAMES = ["x", "w_in", "b_gate", "conv_w", "w_conv_out", "lambda_qk", "subln_g", "w_attn_out", "w_o", "norm_g",
         "w_ff1", "w_ff2"]


def kernel(**inputs):
    import numpy as np
    import concourse.bacc as bacc
    from concourse.bass_utils import run_bass_kernel_spmd

    nc = bacc.Bacc("TRN2", target_bir_lowering=False, num_devices=1)
    arrays, args = {}, []
    for name in NAMES:
        a = np.ascontiguousarray(inputs[name])
        arrays[f"in_{name}"] = a
        args.append(nc.dram_tensor(f"in_{name}", a.shape, mybir.dt.from_np(a.dtype), kind="ExternalInput").ap())
    args.append(nc.dram_tensor("out_0", (1, S, D), F32, kind="ExternalOutput").ap())
    build(nc, *args)
    r = run_bass_kernel_spmd(nc, [arrays], core_ids=[0])
    return r.results[0]["out_0"]
```

```python
from contextlib import ExitStack

import concourse.bass as bass
from concourse import mybir

ALU = mybir.AluOpType
ACT = mybir.ActivationFunctionType
F32 = mybir.dt.float32
F32R = mybir.dt.float32r

P = 128
D = 1024
S = 1024
KT = D // P
TT = S // P
HALF = 512
NH = S // HALF
CONV_K = 3
CT = D // 2 // P
HEADS = 4
HD = D // 16
QB = S // P
FF = 4 * D
FFC = 4
CHUNKS = FF // P // FFC
EPS = 1e-6
LAM_INIT = 0.8 - 0.6
SCALE = HD ** -0.5
SLOPES = [2.0 ** (-8.0 * (h + 1) / HEADS) for h in range(HEADS)]
RING = 2

PAR_G = 0
PAR_B = PAR_G + 4 * KT
PAR_C = PAR_B + 2 * KT
PAR_S = PAR_C + CONV_K * CT
NPAR = PAR_S + 1

COL_H, COL_B, COL_C = 0, CT * P, 2 * CT * P
COL_Q = 3 * CT * P
COL_K = COL_Q + HEADS * P
COL_V = COL_K + HEADS * P
COL_G = COL_V + HEADS * P


def steps(text):
    return [(word[:-1], int(word[-1])) for word in text.split()]


TURN = steps("C7 q0 O0 q1 T7 TL7 k0 AV1 k1 v0 O1 v1 S0 h0 VT0 X0 M0 C0 h1 S1 X1 T0 M1 TL0 C1 c0 S2 X2 T1 M2 "
             "TL1 C2 c1 S3 X3 b0 T2 M3 TL2 C3 b1 S4 X4 g0 T3 M4 TL3 C4 g1 AV0 S5 X5 T4 M5 TL4 C5 g2 S6 X6 T5 "
             "M6 TL5 C6 g3 S7 X7 T6 M7 TL6")
FROM_LAST_HEAD = steps("C7 O0 T7 TL7 AV1 O1")
FIRST_TURN = [x for x in TURN if x not in FROM_LAST_HEAD]
AFTER = [steps("C7 g0 O0 g1 T7 TL7 ZS0 g2 AV1 ZS1 g3 O1 ZS2"), steps("ZS3 OS0 g0 OS1 g1 OS2 g2 OS3 g3")]
PANELS = ["q", "k", "v", "h", "c", "b", "g"]
GATE_PANELS = 2
HEAD_PANELS = len(PANELS) - 1 + GATE_PANELS
HEAD_UNITS = 2 * HEAD_PANELS
GATE_TURNS = 2 * KT // GATE_PANELS
TB = {x: n for n, x in enumerate([x for x in FIRST_TURN if x[0] in ("VT", "T", "AV", "O")]
                                 + [x for x in FROM_LAST_HEAD if x[0] in ("T", "AV", "O")])}
TB_USES = len(TB)

PASSES = ((0, 0), (0, 1), (1, 0))


def unit_of(i, kind, n, after=False):
    if after:
        return i * (2 * GATE_PANELS) + (2 * HEADS * (len(PANELS) - 1) + n)
    return i * HEAD_UNITS + (2 * PANELS.index(kind) + n)


def panel_of(i, kind, n, after=False, ahead=0):
    per, first = (GATE_PANELS, HEADS * (len(PANELS) - 1)) if after else (HEAD_PANELS, PANELS.index(kind))
    j = first + n // 2 + ahead
    return i * per + j, j % RING, i * (per // RING) + j // RING


def tb_use(i, kind, n):
    return (i - ((kind, n) in FROM_LAST_HEAD)) * TB_USES + TB[kind, n]


def one(ap, i):
    return ap[:, bass.ds(i, 1)].rearrange("p o c -> p (o c)")


def build(nc, x, w_in, b_gate, conv_w, w_conv_out, lambda_qk, subln_g, w_attn_out, w_o, norm_g,
          w_ff1, w_ff2, out):
    ctx = ExitStack()

    def sb(name, shape, dt=F32, scope=None):
        return (scope or ctx).enter_context(nc.sbuf_tensor(name, shape, dt))

    def sem(name):
        return ctx.enter_context(nc.semaphore(name))

    with ctx:
        act_hl = [sb("act_hi", [P, KT, S], F32R), sb("act_lo", [P, KT, S], F32R)]
        w_raw = [sb(f"w_raw{s}", [P, KT, P]) for s in range(RING)]
        w_hl = [[sb(f"w_hi{s}", [P, KT, P], F32R), sb(f"w_lo{s}", [P, KT, P], F32R)] for s in range(RING)]
        ident = sb("ident", [P, P])
        ones = sb("ones", [P, P])
        par = sb("par", [P, NPAR + 2])
        gate_bias = sb("gate_bias", [P, GATE_PANELS])
        stats = sb("stats", [P, 2 * TT])
        small = sb("small", [P, 20])
        staging = [sb(f"staging{s}", [P, HALF]) for s in range(2)]
        dev = sb("dev", [P, HALF])
        neg_lam = par[:, NPAR:NPAR + 1]
        sub_gain = par[:, NPAR + 1:NPAR + 2]
        neg_max, exp_sum, recip = small[:, 0:2], small[:, 2:4], small[:, 4:6]
        weight2, eps, spare, maxima = small[:, 6:7], small[:, 7:8], small[:, 8:9], small[:, 10:12]
        dots, dot_exp, lam_diff = small[:, 12:14], small[:, 14:16], small[:, 16:17]

        with ExitStack() as scope:
            z = sb("z", [P, CT, S], scope=scope)
            o = sb("o", [P, HEADS, S], scope=scope)
            with ExitStack() as loop_scope:
                table = sb("alibi", [P, 2 * S - P], scope=loop_scope)
                inner = sb("inner", [P, S + 2], scope=loop_scope)
                with ExitStack() as s1:
                    xn = sb("xn", [P, TT, D], scope=s1)
                    xsq = [sb(f"xsq{s}", [P, D], scope=s1) for s in range(2)]
                    par_rows = sb("par_rows", [NPAR, P], scope=s1)
                    lqk = sb("lqk", [P, 4, HD], scope=s1)
                    lq_junk = sb("lq_junk", [P, HD], scope=s1)
                with ExitStack() as s2:
                    q_st = [sb(f"q_stack{c}", [P, S], F32R, s2) for c in range(2)]
                    k_st = [sb(f"k_stack{c}", [P, S], F32R, s2) for c in range(2)]
                    k_lo = sb("k_lo", [P, S], F32R, s2)
                    v_hl = [sb("v_hi", [P, TT, P], F32R, s2), sb("v_lo", [P, TT, P], F32R, s2)]
                    e = [sb(f"e{c}", [P, S], scope=s2) for c in range(2)]
                    vt = e[1]
                    at_hl = [sb("at_hi", [P, TT, HALF], F32R, s2), sb("at_lo", [P, TT, HALF], F32R, s2)]
            with ExitStack() as s3:
                z_hl = [sb("z_hi", [P, CT, S], F32R, s3), sb("z_lo", [P, CT, S], F32R, s3)]
                o_hl = [sb("o_hi", [P, HEADS, S], F32R, s3), sb("o_lo", [P, HEADS, S], F32R, s3)]
                gate_in = [sb(f"gate_in{s}", [P, 2, HALF], scope=s3) for s in range(2)]
                prod = [sb(f"prod{s}", [P, HALF], scope=s3) for s in range(3)]
        m = sb("m", [P, KT, S])
        with ExitStack() as s4:
            x2 = sb("x2", [P, TT, D], scope=s4)
        acc = sb("acc", [P, KT, S])
        relu = [sb(f"relu{s}", [P, HALF]) for s in range(2)]
        fsq = [sb(f"fsq{s}", [P, HALF]) for s in range(2)]
        ssq = [sb(f"ssq{s}", [P, HALF]) for s in range(2)]
        rstd = sb("rstd", [P, HALF])
        with ExitStack() as s5:
            f_hl = [sb("f_hi", [P, FFC, S], F32R, s5), sb("f_lo", [P, FFC, S], F32R, s5)]
        ost = [sb(f"ost{s}", [P, D]) for s in range(2)]

        psum = ctx.enter_context(nc.psum_tensor("psum", [P, 8, HALF], F32))
        SB, TBK = 2, 6
        gates = nc.dram_tensor("gates_scratch", [2, KT, P, S], F32, kind="Internal").ap()

        x_landed = [sem(f"x_landed{t}") for t in range(TT)]
        par_landed = sem("par_landed")
        setup = sem("setup")
        vec_setup = sem("vector_setup")
        par_t = sem("par_transposed")
        par_ready = sem("par_ready")
        dots_ready = sem("lambda_dots_ready")
        dot_exp_ready = sem("lambda_exp_ready")
        row_sums = [sem(f"row_sums{s}") for s in range(2)]
        row_dev = sem("row_deviations")
        row_rstd = sem("row_rstd")
        xn_ready = sem("x_normed")
        xt_done = sem("x_transposed")
        u_hi = sem("u_hi")
        u_ready = sem("u_ready")
        w_landed = [sem(f"w_landed{s}") for s in range(RING)]
        w_hi = sem("w_hi_ready")
        w_split = sem("w_split")
        proj_done = sem("proj_done")
        qk_hi = sem("qk_hi")
        qk_ready = sem("qk_ready")
        vt_ready = sem("vt_ready")
        h_ready = sem("h_ready")
        c_ready = sem("c_times_h_ready")
        taps = sem("conv_taps")
        z_ready = sem("z_ready")
        bias_ready = sem("gate_bias_ready")
        gate_ready = sem("gate_ready")
        gate_stored = [sem(f"gate_stored{s}") for s in range(2)]
        tb_done = sem("tb_done")
        tb_hi = sem("tb_hi")
        tb_free = sem("tb_free")
        s_done = sem("scores_done")
        s_read = sem("scores_read")
        map1_read = sem("map1_read")
        table_ready = sem("alibi_scaled")
        max_ready = sem("max_ready")
        exp_done = sem("exp_done")
        combine = sem("combine_steps")
        a_ready = sem("a_ready")
        zhi_ready = sem("z_hi_ready")
        zlo_ready = sem("z_lo_ready")
        osq_ready = sem("o_squares_ready")
        odev_ready = sem("o_deviations_ready")
        o_scaled = sem("o_scaled")
        ohi_ready = sem("o_hi_ready")
        olo_ready = sem("o_lo_ready")
        gate_landed = [sem(f"gate_landed{s}") for s in range(2)]
        br_done = sem("branches_done")
        br_read = sem("branches_read")
        merge_steps = sem("merge_steps")
        merged_ready = sem("merged_ready")
        wo_done = sem("wo_done")
        m_ready = sem("m_ready")
        msq_ready = sem("m_squares_ready")
        msq_added = sem("m_squares_added")
        x2_landed = sem("x2_landed")
        msum_done = sem("m_sums_done")
        dev_ready = sem("deviations_ready")
        rstd_ready = sem("rstd_ready")
        res_done = sem("residual_transposed")
        m_scaled = sem("m_scaled")
        h_sum_ready = sem("residual_added")
        sq_ready = sem("squares_ready")
        sq_summed = sem("squares_summed")
        u2_scaled = sem("u2_scaled")
        u2_hi = sem("u2_hi")
        u2_ready = sem("u2_ready")
        ff_done = sem("ff_done")
        relu_done = sem("relu_done")
        fsq_ready = sem("relu_squared")
        fhi_ready = sem("f_hi_ready")
        f_ready = sem("f_ready")
        acc_done = sem("acc_done")
        y_scaled = sem("y_scaled")
        y_ready = sem("y_ready")
        yt_done = sem("y_transposed")
        ost_ready = [sem(f"ost_ready{s}") for s in range(2)]
        stored = [sem(f"stored{s}") for s in range(2)]

        x_tiles = x.rearrange("b (t p) d -> p (b t) d", p=P)
        out_tiles = out.rearrange("b (t p) d -> p (b t) d", p=P)
        w_in_t, w_co_t, w_ao_t, w_o_t, w1_t, w2_t = (
            w.rearrange("l (k p) n -> p (l k) n", p=P) for w in (w_in, w_conv_out, w_attn_out, w_o, w_ff1, w_ff2))

        P_BR = HEADS * (len(PANELS) - 1) + 2 * KT
        P_WO = P_BR + KT
        P_FF = P_WO + KT
        FF_PANELS = FFC + KT // 2
        P_END = P_FF + CHUNKS * FF_PANELS
        GATE_UNITS = 2 * GATE_PANELS
        FF1_UNITS, FF2_UNITS = NH * FFC, NH * KT
        FF_UNITS = FF1_UNITS + FF2_UNITS
        tb_tiles = psum[:, TBK:TBK + 2].rearrange("p b (k c) -> p (b k) c", c=P)
        own = [slice(c * HD, (c + 1) * HD) for c in range(2)]
        other = [own[1], own[0]]
        half_cols = [slice(h * HALF, (h + 1) * HALF) for h in range(NH)]

        def wait(eng, semaphore, value):
            if not isinstance(value, int) or value > 0:
                eng.wait_ge(semaphore, value)

        block = ctx.enter_context(nc.Block())

        @block.sync
        def _(sp):
            def load(panel, slot, *pairs):
                wait(sp, w_split, panel - (RING - 1))
                for dst, src in pairs:
                    sp.dma_start(dst, src).then_inc(w_landed[slot], 32 // len(pairs))

            def w_in_panel(panel, slot, column):
                load(panel, slot, (w_raw[slot][:], w_in_t.rearrange("p k (b c) -> p k b c", c=P)
                                   [:, :, bass.ds(column, 1)].rearrange("p k b c -> p k (b c)")))

            def head_panels(i, js):
                columns = [i + col // P for col in (COL_Q, COL_K, COL_V, COL_H, COL_C, COL_B)]
                columns += [i * GATE_PANELS + (COL_G // P + g) for g in range(GATE_PANELS)]
                for j in js:
                    w_in_panel(i * HEAD_PANELS + j, j % RING, columns[j])

            for h in range(NH):
                for t in range(h * TT // NH, (h + 1) * TT // NH):
                    sp.dma_start(xn[:, t], x_tiles[:, t]).then_inc(x_landed[t], 16)
                head_panels(0, [h])
            head_panels(0, range(NH, HEAD_PANELS))
            with sp.Fori(1, HEADS) as i:
                head_panels(i, range(HEAD_PANELS))
            with sp.Fori(HEADS, GATE_TURNS) as i:
                for g in range(GATE_PANELS):
                    w_in_panel(i * GATE_PANELS + (P_BR - 2 * KT + g), g % RING, i * GATE_PANELS + (COL_G // P + g))
            def branch_panels(i):
                for j in range(RING):
                    cols = bass.ds(i * (RING * P) + j * P, P)
                    load(i * RING + (P_BR + j), j, (w_raw[j][:, 0:CT], w_co_t[:, :, cols]),
                         (w_raw[j][:, CT:KT], w_ao_t[:, :, cols]))
                    for h in range(NH):
                        if isinstance(i, int):
                            sp.wait_ge(gate_stored[h], 16 * (KT + i * RING + j + 1))
                        sp.wait_ge(br_read, i * (4 * RING) + 4 * j + 2 * h + 2)
                        sp.dma_start(gate_in[h][:], gates[:, bass.ds(i * RING + j, 1), :, half_cols[h]]
                                     .rearrange("b o p c -> p (b o) c")).then_inc(gate_landed[h], 16)

            branch_panels(0)
            for h in range(NH):
                sp.wait_ge(gate_stored[h], 16 * 2 * KT)
            with sp.Fori(1, KT // RING) as i:
                branch_panels(i)
            with sp.Fori(0, KT // RING) as i:
                for j in range(RING):
                    load(i * RING + (P_WO + j), j, (w_raw[j][:], w_o_t[:, :, bass.ds(i * (RING * P) + j * P, P)]))
            sp.wait_ge(br_done, 4 * KT)
            for t in range(TT):
                sp.dma_start(x2[:, t], x_tiles[:, t]).then_inc(x2_landed, 16)
            with sp.Fori(0, CHUNKS) as i:
                for j in range(FFC):
                    load(i * FF_PANELS + (P_FF + j), j % RING,
                         (w_raw[j % RING][:], w1_t[:, :, bass.ds(i * (FFC * P) + j * P, P)]))
                for j in range(KT // 2):
                    slot = (FFC + j) % RING
                    load(i * FF_PANELS + (P_FF + FFC + j), slot,
                         (w_raw[slot][:].rearrange("p (k d) c -> p k (d c)", d=2),
                          w2_t[:, bass.ds(i * FFC, FFC), j * 2 * P:(j + 1) * 2 * P]))
            for t in range(TT):
                sp.wait_ge(ost_ready[t % 2], 2 * (t // 2 + 1))
                sp.dma_start(out_tiles[:, t], ost[t % 2][:]).then_inc(stored[t % 2], 16)
            for s in range(2):
                sp.wait_ge(stored[s], 16 * (TT // 2))

        @block.gpsimd
        def _(pool):
            nc.gpsimd.memset(ident[:], 1.0).then_inc(setup, 1)
            pool.wait_ge(setup, 1)
            nc.gpsimd.affine_select(out=ident[:], in_=ident[:], compare_op=ALU.is_equal, fill=0.0, base=0,
                                    pattern=[[-1, P]], channel_multiplier=1).then_inc(setup, 1)
            nc.gpsimd.memset(ones[:], 1.0).then_inc(setup, 1)
            nc.gpsimd.iota(table[:], [[-1, 2 * S - P]], base=S - P, channel_multiplier=1,
                           allow_small_or_imprecise_dtypes=True).then_inc(setup, 1)
            nc.gpsimd.memset(inner[:], 0.0).then_inc(setup, 1)
            pool.wait_ge(wo_done, 1)
            for h in range(NH):
                nc.gpsimd.memset(ssq[h][:], 0.0).then_inc(msq_added, 1)
            pool.wait_ge(msq_added, NH)
            with pool.Fori(0, KT) as i:
                for h in range(NH):
                    pool.wait_ge(msq_ready, i * NH + (h + 1))
                    pool.wait_ge(msq_added, i * NH + (h + NH - 1))
                    nc.gpsimd.tensor_tensor(ssq[h][:], ssq[h][:], fsq[h][:], ALU.add).then_inc(msq_added, 1)
            pool.wait_ge(res_done, NH * KT)
            nc.gpsimd.memset(acc[:], 0.0).then_inc(acc_done, FF2_UNITS)

        @block.tensor
        def _(pe):
            pe.sem_inc(m_ready, 2)
            pe.sem_inc(f_ready, 2)

            def product(bank, stat, moving, kts):
                terms = [(kt, a, b) for kt in kts for a, b in PASSES]
                for t, (kt, a, b) in enumerate(terms):
                    mm = nc.tensor.matmul(bank, stat(a, kt), moving(b, kt), start=(t == 0),
                                          stop=(t == len(terms) - 1))
                return mm

            pe.wait_ge(par_landed, 16 * 5)
            pe.wait_ge(setup, 3)
            nc.tensor.transpose(psum[:, 7, 0:NPAR], par_rows[:], ident[0:NPAR, 0:NPAR]).then_inc(par_t, 1)

            def turn_x(h):
                pe.wait_ge(xn_ready, (h + 1) * (TT // NH))
                for kt in range(KT):
                    n = h * KT + kt
                    wait(pe, u_ready, n - 3)
                    for t in range(4):
                        mm = nc.tensor.transpose(psum[:, SB + n % 4, t * P:(t + 1) * P],
                                                 xn[:, 4 * h + t, kt * P:(kt + 1) * P], ident[:])
                    mm.then_inc(xt_done, 1)

            def walk(i, steps, after=False):
                for kind, n in steps:
                    if kind in PANELS:
                        h = n % NH
                        panel, slot, _ = panel_of(i, kind, n, after)
                        if h == 0:
                            pe.wait_ge(w_split, panel + 1)
                        if kind == "q":
                            wait(pe, gate_ready, i * GATE_UNITS - (1 - h))
                        elif kind == "k":
                            pe.wait_ge(qk_ready, i * 4 + (1 + h))
                        elif kind == "v":
                            pe.wait_ge(qk_ready, i * 4 + (3 + h))
                        elif kind == "h":
                            pe.wait_ge(vt_ready, i * 2 + (1 + h))
                        elif kind == "c":
                            pe.wait_ge(h_ready, i * 2 + (1 + h))
                        elif kind == "b":
                            pe.wait_ge(c_ready, i * 2 + (1 + h))
                        elif n < 2 and not after:
                            pe.wait_ge(z_ready, i * 2 + (1 + h))
                        else:
                            pe.wait_ge(gate_ready, i * GATE_UNITS + (n - 1))
                        product(psum[:, h], lambda a, kt: w_hl[slot][a][:, kt],
                                lambda b, kt: act_hl[b][:, kt, half_cols[h]], range(KT)).then_inc(proj_done, 1)
                    elif kind == "S":
                        if n == 0:
                            pe.wait_ge(qk_ready, i * 4 + 4)
                        wait(pe, s_read, i * QB + n)
                        for c in range(2):
                            for half in range(NH):
                                nc.tensor.matmul(psum[:, SB + 2 * c + half], q_st[c][:, n * P:(n + 1) * P],
                                                 k_st[c][:, half_cols[half]], start=True, stop=False)
                        for half in range(NH):
                            for c in range(2):
                                mm = nc.tensor.matmul(psum[:, SB + 2 * c + half], q_st[c][own[c], n * P:(n + 1) * P],
                                                      k_lo[own[c], half_cols[half]], start=False, stop=True)
                        mm.then_inc(s_done, 1)
                    elif kind in ("VT", "T"):
                        if kind == "VT":
                            pe.wait_ge(vt_ready, i * 2 + 2)
                        else:
                            pe.wait_ge(a_ready, i * QB + (n + 1 if n < 7 else 0))
                        wait(pe, tb_free, tb_use(i, kind, n))
                        src = vt if kind == "VT" else e[0]
                        for k in range(TT):
                            mm = nc.tensor.transpose(psum[:, TBK + k // 4, (k % 4) * P:(k % 4 + 1) * P],
                                                     src[:, k * P:(k + 1) * P], ident[:])
                        mm.then_inc(tb_done, 1)
                    elif kind == "AV":
                        pe.wait_ge(tb_free, tb_use(i, kind, n))
                        product(psum[:, TBK], lambda a, kt: v_hl[a][:, kt], lambda b, kt: at_hl[b][:, kt],
                                range(TT)).then_inc(tb_done, 1)
                    elif kind == "O":
                        pe.wait_ge(osq_ready, i * 2 + (n - 1))
                        pe.wait_ge(tb_free, tb_use(i, kind, n))
                        nc.tensor.matmul(psum[:, TBK], ones[:], dev[:], start=True, stop=True).then_inc(tb_done, 1)

            turn_x(0)
            pe.wait_ge(u_ready, KT)
            walk(0, FIRST_TURN[:1])
            turn_x(1)
            pe.wait_ge(u_ready, NH * KT)
            walk(0, FIRST_TURN[1:])
            with pe.Fori(1, HEADS) as i:
                walk(i, TURN)
            walk(HEADS, AFTER[0], True)
            pe.wait_ge(s_read, HEADS * QB)
            pe.wait_ge(tb_free, HEADS * TB_USES)
            pe.sem_inc(br_read, 4)
            walk(HEADS + 1, AFTER[1], True)
            with pe.Fori(HEADS + len(AFTER), GATE_TURNS) as i:
                walk(i, [("g", n) for n in range(GATE_UNITS)], True)

            pe.wait_ge(gate_ready, GATE_TURNS * GATE_UNITS)
            pe.wait_ge(zlo_ready, CT)
            pe.wait_ge(olo_ready, HEADS)
            with pe.Fori(0, KT // RING) as i:
                for j in range(RING):
                    pe.wait_ge(w_split, i * RING + (P_BR + j + 1))
                    for h in range(NH):
                        for br in range(2):
                            pe.wait_ge(br_read, i * (4 * RING) + (4 * j + 2 * h + br + 1))
                            src = (z_hl, o_hl)[br]
                            product(psum[:, 2 * h + br], lambda a, kt: w_hl[j][a][:, CT * br + kt],
                                    lambda b, kt: src[b][:, kt, half_cols[h]], range(CT)).then_inc(br_done, 1)

            pe.wait_ge(br_read, 4 * KT + 4)
            pe.wait_ge(merged_ready, NH * KT)
            with pe.Fori(0, KT // RING) as i:
                for j in range(RING):
                    pe.wait_ge(w_split, i * RING + (P_WO + j + 1))
                    for h in range(NH):
                        pe.wait_ge(m_ready, i * (RING * NH) + (NH * j + h + 1))
                        product(psum[:, h], lambda a, kt: w_hl[j][a][:, kt],
                                lambda b, kt: act_hl[b][:, kt, half_cols[h]], range(KT)).then_inc(wo_done, 1)

            pe.wait_ge(x2_landed, 16 * TT)
            pe.wait_ge(msq_added, NH + NH * KT)
            pe.wait_ge(m_ready, NH * KT + 2)
            for h in range(NH):
                nc.tensor.matmul(psum[:, 4], ones[:], ssq[h][:], start=True, stop=True).then_inc(msum_done, 1)
                for kt in range(KT):
                    n = h * KT + kt
                    wait(pe, h_sum_ready, n - 3)
                    for t in range(4):
                        mm = nc.tensor.transpose(psum[:, n % 4, t * P:(t + 1) * P],
                                                 x2[:, 4 * h + t, kt * P:(kt + 1) * P], ident[:])
                    mm.then_inc(res_done, 1)
                for kt in range(KT):
                    n = h * KT + kt
                    pe.wait_ge(sq_ready, n + 1)
                    nc.tensor.matmul(psum[:, 5], ones[:], fsq[n % 2][:], start=(kt == 0), stop=(kt == KT - 1)
                                     ).then_inc(sq_summed, 1)
                pe.wait_ge(dev_ready, 2 * h + 2)

            pe.wait_ge(h_sum_ready, NH * KT)
            pe.wait_ge(u2_ready, NH * KT)
            with pe.Fori(0, CHUNKS) as i:
                for j in range(FFC):
                    pe.wait_ge(w_split, i * FF_PANELS + (P_FF + j + 1))
                    for h in range(NH):
                        u = NH * j + h
                        if u < 4:
                            pe.wait_ge(acc_done, i * FF2_UNITS + (FF2_UNITS - 3 + u))
                        else:
                            pe.wait_ge(relu_done, i * FF1_UNITS + (u - 3))
                        product(psum[:, u % 4], lambda a, kt: w_hl[j % RING][a][:, kt],
                                lambda b, kt: act_hl[b][:, kt, half_cols[h]], range(KT)).then_inc(ff_done, 1)
                for j in range(KT // 2):
                    slot = (FFC + j) % RING
                    pe.wait_ge(w_split, i * FF_PANELS + (P_FF + FFC + j + 1))
                    for dd in range(2):
                        for h in range(NH):
                            u = 4 * j + 2 * dd + h
                            if u < NH:
                                pe.wait_ge(f_ready, i * FF1_UNITS + (2 + FF1_UNITS - 1 + h))
                            if u < 4:
                                pe.wait_ge(relu_done, i * FF1_UNITS + (FF1_UNITS - 3 + u))
                            else:
                                pe.wait_ge(acc_done, i * FF2_UNITS + (FF2_UNITS + u - 3))
                            product(psum[:, u % 4], lambda a, kt: w_hl[slot][a][:, 2 * kt + dd],
                                    lambda b, kt: f_hl[b][:, kt, half_cols[h]], range(FFC)).then_inc(ff_done, 1)

            for h in range(NH):
                for kt in range(KT):
                    n = (NH + h) * KT + kt
                    pe.wait_ge(sq_ready, n + 1)
                    nc.tensor.matmul(psum[:, 6 + h], ones[:], fsq[n % 2][:], start=(kt == 0), stop=(kt == KT - 1)
                                     ).then_inc(sq_summed, 1)
            pe.wait_ge(acc_done, (CHUNKS + 1) * FF2_UNITS)
            for t in range(TT):
                if t % 4 == 0:
                    pe.wait_ge(y_ready, KT * (t // 4 + 1))
                wait(pe, ost_ready[t % 2], 2 * (t // 2))
                for kt in range(KT):
                    mm = nc.tensor.transpose(psum[:, 2 * (t % 2) + kt // 4, (kt % 4) * P:(kt % 4 + 1) * P],
                                             m[:, kt, t * P:(t + 1) * P], ident[:])
                mm.then_inc(yt_done, 1)

        @block.scalar
        def _(act):
            for src, a, b in ((norm_g, PAR_G, PAR_B), (b_gate, PAR_B, PAR_C), (conv_w, PAR_C, PAR_S)):
                act.dma_start(par_rows[a:b, :], src.rearrange("l n (k c) -> (l n k) c", c=P)).then_inc(par_landed, 16)
            act.dma_start(par_rows[PAR_S:NPAR, :], subln_g).then_inc(par_landed, 16)
            act.dma_start(lqk[:].rearrange("p n c -> p (n c)"),
                          lambda_qk.rearrange("l n c -> l (n c)").to_broadcast([P, 4 * HD])).then_inc(par_landed, 16)

            def split_hi(panel, slot, turns):
                act.wait_ge(w_landed[slot], turns * 32 + 32)
                nc.scalar.activation(w_hl[slot][0][:], w_raw[slot][:], ACT.Copy).then_inc(w_hi, 1)

            def squares(n, src):
                wait(act, sq_summed, n - 1)
                nc.scalar.activation(fsq[n % 2][:], src, ACT.Square).then_inc(sq_ready, 1)

            act.wait_ge(dots_ready, 2)
            nc.scalar.activation(dot_exp, dots, ACT.Exp).then_inc(dot_exp_ready, 1)
            act.wait_ge(vec_setup, 1)
            for h in range(NH):
                for t in range(4 * h, 4 * h + 4, 2):
                    act.wait_ge(x_landed[t], 16)
                    wait(act, row_sums[0], t // 2)
                    nc.scalar.activation(xsq[0][:], xn[:, t], ACT.Square, accum_out=stats[:, t:t + 1]
                                         ).then_inc(row_sums[0], 1)
                for s in range(2):
                    act.wait_ge(row_sums[s], 2 * h + 2)
                nc.scalar.activation(stats[:, TT + 4 * h:TT + 4 * h + 4], stats[:, 4 * h:4 * h + 4], ACT.Sqrt,
                                     bias=eps, scale=1.0 / D).then_inc(row_dev, 1)
                if h == 0:
                    split_hi(0, 0, 0)
                    act.wait_ge(par_ready, 1)
                for kt in range(KT):
                    n = h * KT + kt
                    act.wait_ge(xt_done, n + 1)
                    nc.scalar.activation(act_hl[0][:, kt, half_cols[h]], psum[:, SB + n % 4], ACT.Copy,
                                         scale=par[:, PAR_G + kt:PAR_G + kt + 1]).then_inc(u_hi, 1)
            nc.scalar.preload_act_table(ACT.Exp)

            def walk(i, steps, after=False):
                for kind, n in steps:
                    if kind in PANELS:
                        h = n % NH
                        if kind not in "cb" or h == 0:
                            act.wait_ge(proj_done, unit_of(i, kind, n, after) + 1)
                        if kind == "q":
                            for c in range(2):
                                ins = nc.scalar.activation(q_st[c][own[c], half_cols[h]], psum[own[c], h], ACT.Copy)
                            ins.then_inc(qk_hi, 1)
                        elif kind == "k":
                            for c in range(2):
                                for rows in (own[c], other[c]):
                                    ins = nc.scalar.activation(k_st[c][rows, half_cols[h]], psum[own[c], h], ACT.Copy)
                            ins.then_inc(qk_hi, 1)
                        elif kind == "v":
                            wait(act, a_ready, i * QB)
                            nc.scalar.activation(vt[:, half_cols[h]], psum[:, h], ACT.Copy).then_inc(vt_ready, 1)
                        elif kind == "h":
                            nc.scalar.activation(inner[:, 1 + h * HALF:1 + (h + 1) * HALF], psum[:, h], ACT.Copy
                                                 ).then_inc(h_ready, 1)
                        elif kind == "g":
                            if n == 0:
                                act.wait_ge(bias_ready, i + 1)
                            wait(act, gate_stored[h], i * (16 * GATE_PANELS) + 16 * (n // 2))
                            nc.scalar.activation(staging[h][:], psum[:, h], ACT.Tanh, scale=0.5,
                                                 bias=gate_bias[:, n // 2:n // 2 + 1]).then_inc(gate_ready, 1)
                            act.wait_ge(gate_ready, i * GATE_UNITS + (n + 1))
                            act.dma_start(one(gates.rearrange("b k p s -> p (b k) s"), i * GATE_PANELS + n // 2)
                                          [:, half_cols[h]], staging[h][:]).then_inc(gate_stored[h], 16)
                        if h == 0:
                            split_hi(*panel_of(i, kind, n, after, 1))
                    elif kind in "XM":
                        c = "MX".index(kind)
                        act.wait_ge(max_ready, i * (2 * QB) + (2 * n + 2 - c))
                        nc.scalar.activation(e[c][:], e[c][:], ACT.Exp, scale=SCALE, bias=neg_max[:, c:c + 1],
                                             accum_out=exp_sum[:, c:c + 1]).then_inc(exp_done, 1)
                    elif kind in ("VT", "T"):
                        act.wait_ge(tb_done, tb_use(i, kind, n) + 1)
                        dst = v_hl[0][:] if kind == "VT" else at_hl[0][:, :, (n % 4) * P:(n % 4 + 1) * P]
                        nc.scalar.activation(dst, tb_tiles, ACT.Copy).then_inc(tb_hi, 1)
                    elif kind == "AV":
                        wait(act, o_scaled, i * 2 - n)
                        act.wait_ge(tb_done, tb_use(i, kind, n) + 1)
                        nc.scalar.activation(dev[:], psum[:, TBK], ACT.Square).then_inc(osq_ready, 1)
                    elif kind == "O":
                        act.wait_ge(tb_done, tb_use(i, kind, n) + 1)
                        nc.scalar.activation(dev[:], psum[:, TBK], ACT.Sqrt, bias=eps, scale=1.0 / (2 * HD)
                                             ).then_inc(odev_ready, 1)
                    elif kind == "ZS":
                        act.wait_ge(z_ready, NH * HEADS)
                        act.wait_ge(s_read, QB * HEADS)
                        nc.scalar.activation(z_hl[0][:, n], z[:, n], ACT.Copy).then_inc(zhi_ready, 1)
                    elif kind == "OS":
                        act.wait_ge(tb_free, HEADS * TB_USES)
                        act.wait_ge(o_scaled, 2 * n + 2)
                        nc.scalar.activation(o_hl[0][:, n], o[:, n], ACT.Copy).then_inc(ohi_ready, 1)

            walk(0, FIRST_TURN)
            with act.Fori(1, HEADS) as i:
                walk(i, TURN)
            for n, steps in enumerate(AFTER):
                walk(HEADS + n, steps, True)
            nc.scalar.preload_act_table(ACT.Tanh)
            with act.Fori(HEADS + len(AFTER), GATE_TURNS) as i:
                walk(i, [("g", n) for n in range(GATE_UNITS)], True)
            nc.scalar.preload_act_table(ACT.Sqrt)

            with act.Fori(0, KT // RING) as i:
                for j in range(RING):
                    act.wait_ge(br_done, i * (4 * RING) + (4 * j + 1))
                    split_hi(i * RING + (P_BR + j + 1), (j + 1) % RING, i + (P_BR + j + 1) // RING)
            with act.Fori(0, KT // RING) as i:
                for j in range(RING):
                    for h in range(NH):
                        n = NH * j + h
                        act.wait_ge(wo_done, i * (RING * NH) + (n + 1))
                        act.wait_ge(msq_added, i * (RING * NH) + (n + 1))
                        nc.scalar.activation(fsq[h][:], psum[:, h], ACT.Square).then_inc(msq_ready, 1)
                        if h == 0:
                            split_hi(i * RING + (P_WO + j + 1), (j + 1) % RING, i + (P_WO + j + 1) // RING)

            act.wait_ge(msq_added, NH + NH * KT)
            for h in range(NH):
                act.wait_ge(msum_done, h + 1)
                wait(act, rstd_ready, 2 * h)
                nc.scalar.activation(dev[:], psum[:, 4], ACT.Sqrt, bias=eps, scale=1.0 / D).then_inc(dev_ready, 1)
                for kt in range(KT):
                    n = h * KT + kt
                    act.wait_ge(h_sum_ready, n + 1)
                    squares(n, m[:, kt, half_cols[h]])
                act.wait_ge(sq_summed, (h + 1) * KT)
                act.wait_ge(rstd_ready, 2 * h + 1)
                nc.scalar.activation(dev[:], psum[:, 5], ACT.Sqrt, bias=eps, scale=1.0 / D).then_inc(dev_ready, 1)
                for kt in range(KT):
                    n = h * KT + kt
                    act.wait_ge(u2_scaled, n + 1)
                    nc.scalar.activation(act_hl[0][:, kt, half_cols[h]], relu[n % 2][:], ACT.Copy
                                         ).then_inc(u2_hi, 1)

            def chunk(i, last):
                for j in range(FF_PANELS):
                    if j < FFC:
                        for h in range(NH):
                            u = NH * j + h
                            act.wait_ge(ff_done, i * FF_UNITS + (u + 1))
                            nc.scalar.activation(relu[h][:], psum[:, u % 4], ACT.Relu).then_inc(relu_done, 1)
                            if h == 0:
                                split_hi(i * FF_PANELS + (P_FF + j + 1), (j + 1) % RING,
                                         i * (FF_PANELS // RING) + (P_FF + j + 1) // RING)
                            act.wait_ge(relu_done, i * FF1_UNITS + (u + 1))
                            act.wait_ge(f_ready, i * FF1_UNITS + (u + 1))
                            nc.scalar.activation(fsq[h][:], relu[h][:], ACT.Square).then_inc(fsq_ready, 1)
                    elif not (last and j == FF_PANELS - 1):
                        act.wait_ge(ff_done, i * FF_UNITS + (FF1_UNITS + 4 * (j - FFC) + 1))
                        split_hi(i * FF_PANELS + (P_FF + j + 1), (j + 1) % RING,
                                 i * (FF_PANELS // RING) + (P_FF + j + 1) // RING)

            with act.Fori(0, CHUNKS - 1) as i:
                chunk(i, False)
            chunk(CHUNKS - 1, True)

            act.wait_ge(acc_done, (CHUNKS + 1) * FF2_UNITS)
            act.wait_ge(f_ready, 2 + CHUNKS * FF1_UNITS)
            for h in range(NH):
                for kt in range(KT):
                    squares((NH + h) * KT + kt, acc[:, kt, half_cols[h]])
                act.wait_ge(sq_summed, (NH + h + 1) * KT)
                act.wait_ge(rstd_ready, 2 * NH + h)
                nc.scalar.activation(dev[:], psum[:, 6 + h], ACT.Sqrt, bias=eps, scale=1.0 / D
                                     ).then_inc(dev_ready, 1)
            for t in range(TT):
                act.wait_ge(yt_done, t + 1)
                wait(act, stored[t % 2], 16 * (t // 2))
                nc.scalar.activation(ost[t % 2][:, 0:HALF], psum[:, 2 * (t % 2)], ACT.Copy
                                     ).then_inc(ost_ready[t % 2], 1)

        @block.vector
        def _(dve):
            vec = nc.vector

            def lo_part(dst_hl, idx, src, semaphore, gain=None):
                hi, lo = dst_hl[0][idx].bitcast(F32), dst_hl[1][idx]
                if gain is None:
                    return vec.tensor_tensor(lo, src, hi, ALU.subtract).then_inc(semaphore, 1)
                return vec.scalar_tensor_tensor(out=lo, in0=src, scalar=gain, in1=hi, op0=ALU.mult,
                                                op1=ALU.subtract).then_inc(semaphore, 1)

            def split_lo(panel, slot):
                dve.wait_ge(w_hi, panel + 1)
                vec.tensor_tensor(w_hl[slot][1][:], w_raw[slot][:], w_hl[slot][0][:].bitcast(F32), ALU.subtract
                                  ).then_inc(w_split, 1)

            vec.memset(eps, EPS).then_inc(vec_setup, 1)
            dve.wait_ge(par_landed, 16 * 5)
            for c in range(2):
                wait(dve, dots_ready, c)
                vec.tensor_tensor_reduce(out=lq_junk[:], in0=lqk[:, 2 * c], in1=lqk[:, 2 * c + 1], scale=1.0,
                                         scalar=0.0, op0=ALU.mult, op1=ALU.add, accum_out=dots[:, c:c + 1]
                                         ).then_inc(dots_ready, 1)
            dve.wait_ge(par_t, 1)
            vec.tensor_copy(par[:, 0:NPAR], psum[:, 7, 0:NPAR]).then_inc(par_ready, 1)
            dve.wait_ge(par_ready, 1)
            vec.tensor_scalar(sub_gain, par[:, PAR_S:NPAR], 1.0 - LAM_INIT, None, ALU.mult).then_inc(vec_setup, 1)
            dve.wait_ge(setup, 5)
            vec.scalar_tensor_tensor(out=table[:], in0=table[:], scalar=-1.0, in1=table[:], op0=ALU.mult,
                                     op1=ALU.min).then_inc(vec_setup, 1)
            dve.wait_ge(vec_setup, 3)
            vec.tensor_scalar(table[:], table[:], SLOPES[0] / SCALE, None, ALU.mult).then_inc(table_ready, 1)
            dve.wait_ge(dot_exp_ready, 1)
            vec.tensor_tensor(lam_diff, dot_exp[:, 1:2], dot_exp[:, 0:1], ALU.subtract).then_inc(vec_setup, 1)
            dve.wait_ge(vec_setup, 4)
            vec.tensor_scalar(neg_lam, lam_diff, -LAM_INIT, None, ALU.add).then_inc(vec_setup, 1)
            for h in range(NH):
                for t in range(4 * h + 1, 4 * h + 4, 2):
                    dve.wait_ge(x_landed[t], 16)
                    wait(dve, row_sums[1], t // 2)
                    vec.tensor_tensor_reduce(out=xsq[1][:], in0=xn[:, t], in1=xn[:, t], scale=1.0, scalar=0.0,
                                             op0=ALU.mult, op1=ALU.add, accum_out=stats[:, t:t + 1]
                                             ).then_inc(row_sums[1], 1)
                dve.wait_ge(row_dev, h + 1)
                cols = slice(TT + 4 * h, TT + 4 * h + 4)
                vec.reciprocal(stats[:, cols], stats[:, cols]).then_inc(row_rstd, 1)
                dve.wait_ge(row_rstd, h + 1)
                for t in range(4 * h, 4 * h + 4):
                    vec.tensor_scalar(xn[:, t], xn[:, t], stats[:, TT + t:TT + t + 1], None, ALU.mult
                                      ).then_inc(xn_ready, 1)
                if h == 0:
                    split_lo(0, 0)
                for kt in range(KT):
                    n = h * KT + kt
                    dve.wait_ge(u_hi, n + 1)
                    lo_part(act_hl, (slice(None), kt, half_cols[h]), psum[:, SB + n % 4], u_ready,
                            par[:, PAR_G + kt:PAR_G + kt + 1])

            def walk(i, steps, after=False):
                for kind, n in steps:
                    if kind in PANELS:
                        h = n % NH
                        u = unit_of(i, kind, n, after)
                        cols = half_cols[h]
                        if kind in "qk":
                            dve.wait_ge(qk_hi, i * 4 + (2 * "qk".index(kind) + h + 1))
                            for c in range(2):
                                hi = (q_st if kind == "q" else k_st)[c][own[c], cols].bitcast(F32)
                                lo = q_st[c][other[c], cols] if kind == "q" else k_lo[own[c], cols]
                                ins = vec.tensor_tensor(lo, psum[own[c], h], hi, ALU.subtract)
                            ins.then_inc(qk_ready, 1)
                        elif kind == "c":
                            dve.wait_ge(proj_done, u + 1)
                            dve.wait_ge(h_ready, i * 2 + (h + 1))
                            span = inner[:, 1 + h * HALF:1 + (h + 1) * HALF]
                            vec.tensor_tensor(span, psum[:, h], span, ALU.mult).then_inc(c_ready, 1)
                            if h == 1:
                                for tap in range(CONV_K):
                                    wc = par[:, bass.ds(i + (PAR_C + tap * CT), 1)]
                                    win = inner[:, tap:tap + S]
                                    if tap == 0:
                                        dve.wait_ge(c_ready, i * 2 + 2)
                                        vec.tensor_scalar(one(z, i), win, wc, None, ALU.mult).then_inc(taps, 1)
                                    else:
                                        dve.wait_ge(taps, i * CONV_K + tap)
                                        vec.scalar_tensor_tensor(out=one(z, i), in0=win, scalar=wc, in1=one(z, i),
                                                                 op0=ALU.mult, op1=ALU.add).then_inc(taps, 1)
                        elif kind == "b":
                            dve.wait_ge(proj_done, u + 1)
                            dve.wait_ge(taps, i * CONV_K + CONV_K)
                            vec.tensor_tensor(one(z, i)[:, cols], psum[:, h], one(z, i)[:, cols], ALU.mult
                                              ).then_inc(z_ready, 1)
                        if (kind, n) == (("g", 0) if after else ("c", 0)):
                            wait(dve, gate_ready, i * GATE_UNITS)
                            vec.tensor_scalar(gate_bias[:], par[:, bass.ds(i * GATE_PANELS + PAR_B, GATE_PANELS)], 0.5,
                                              None, ALU.mult).then_inc(bias_ready, 1)
                        if h == 0:
                            split_lo(*panel_of(i, kind, n, after, 1)[:2])
                    elif kind in "XM":
                        c = "MX".index(kind)
                        if (kind, n) == ("X", 0) and not isinstance(i, int):
                            vec.tensor_scalar(table[:], table[:], SLOPES[1] / SLOPES[0], None, ALU.mult
                                              ).then_inc(table_ready, 1)
                        if (kind, n) == ("X", 0):
                            dve.wait_ge(table_ready, i + 1)
                        if kind == "X":
                            dve.wait_ge(s_done, i * QB + (n + 1))
                            if n > 0:
                                dve.wait_ge(a_ready, i * QB + n)
                        elif n > 0:
                            dve.wait_ge(tb_done, tb_use(i, "T", n - 1) + 1)
                        vec.memset(spare, 0.0)
                        start = S - P - P * n
                        read = (s_read, map1_read)[c]
                        vec.tensor_tensor_reduce(
                            out=e[c][:], in0=psum[:, SB + 2 * c:SB + 2 * c + 2].rearrange("p b c -> p (b c)"),
                            in1=table[:, start:start + S], scale=1.0, scalar=-3.0e38, op0=ALU.add, op1=ALU.max,
                            accum_out=maxima[:, c:c + 1]).then_inc(read, 1)
                        dve.wait_ge(read, i * QB + (n + 1))
                        vec.tensor_scalar(neg_max[:, c:c + 1], maxima[:, c:c + 1], -SCALE, None, ALU.mult
                                          ).then_inc(max_ready, 1)
                    elif kind == "C":
                        blk = i * QB + (n if n < 7 else -1)
                        dve.wait_ge(exp_done, blk * 2 + 2)
                        vec.reciprocal(recip, exp_sum).then_inc(combine, 1)
                        dve.wait_ge(combine, blk * 3 + 1)
                        vec.tensor_scalar(weight2, recip[:, 1:2], neg_lam, None, ALU.mult).then_inc(combine, 1)
                        dve.wait_ge(combine, blk * 3 + 2)
                        vec.tensor_scalar(e[1][:], e[1][:], weight2, None, ALU.mult).then_inc(combine, 1)
                        dve.wait_ge(combine, blk * 3 + 3)
                        vec.scalar_tensor_tensor(out=e[0][:], in0=e[0][:], scalar=recip[:, 0:1], in1=e[1][:],
                                                 op0=ALU.mult, op1=ALU.add).then_inc(a_ready, 1)
                    elif kind in ("VT", "TL"):
                        dve.wait_ge(tb_hi, i * (QB + 1) + {"VT": 1, "TL": 2 + n if n < 7 else 0}[kind])
                        if kind == "VT":
                            lo_part(v_hl, slice(None), tb_tiles, tb_free)
                        else:
                            lo_part(at_hl, (slice(None), slice(None), slice((n % 4) * P, (n % 4 + 1) * P)), tb_tiles,
                                    tb_free)
                    elif kind == "AV":
                        dve.wait_ge(osq_ready, i * 2 - n + 1)
                        vec.tensor_scalar(one(o, i - n)[:, half_cols[n]], psum[:, TBK], 1.0, None, ALU.mult
                                          ).then_inc(tb_free, 1)
                    elif kind == "O":
                        k = i * 2 + (n - 2)
                        dve.wait_ge(odev_ready, k + 1)
                        vec.reciprocal(dev[:], dev[:]).then_inc(tb_free, 1)
                        dve.wait_ge(tb_free, tb_use(i, kind, n) + 1)
                        span = one(o, i - 1)[:, half_cols[n]]
                        vec.scalar_tensor_tensor(out=span, in0=span, scalar=sub_gain, in1=dev[:], op0=ALU.mult,
                                                 op1=ALU.mult).then_inc(o_scaled, 1)
                    elif kind == "ZS":
                        dve.wait_ge(zhi_ready, n + 1)
                        lo_part(z_hl, (slice(None), n), z[:, n], zlo_ready)
                    elif kind == "OS":
                        dve.wait_ge(ohi_ready, n + 1)
                        lo_part(o_hl, (slice(None), n), o[:, n], olo_ready)

            walk(0, FIRST_TURN)
            with dve.Fori(1, HEADS) as i:
                walk(i, TURN)
            for n, steps in enumerate(AFTER):
                walk(HEADS + n, steps, True)
            with dve.Fori(HEADS + len(AFTER), GATE_TURNS) as i:
                walk(i, [("g", n) for n in range(GATE_UNITS)], True)

            with dve.Fori(0, KT // RING) as i:
                for j in range(RING):
                    for h in range(NH):
                        n = NH * j + h
                        for br in range(2):
                            if br == 0:
                                dve.wait_ge(gate_landed[h], i * (16 * RING) + 16 * (j + 1))
                            dve.wait_ge(br_done, i * (4 * RING) + (2 * n + br + 1))
                            vec.scalar_tensor_tensor(out=prod[br][:], in0=gate_in[h][:, br], scalar=1.0,
                                                     in1=psum[:, 2 * h + br], op0=ALU.add, op1=ALU.mult
                                                     ).then_inc(br_read, 1)
                            if br == 0 and h == 0:
                                split_lo(i * RING + (P_BR + j + 1), (j + 1) % RING)
                        dve.wait_ge(br_read, i * (4 * RING) + (4 + 2 * n + 2))
                        vec.tensor_tensor(prod[2][:], prod[0][:], prod[1][:], ALU.add).then_inc(merge_steps, 1)
                        hi = one(act_hl[0], i * RING + j)[:, half_cols[h]]
                        lo = one(act_hl[1], i * RING + j)[:, half_cols[h]]
                        dve.wait_ge(merge_steps, i * (4 * RING) + (2 * n + 1))
                        vec.tensor_scalar(hi, prod[2][:], 0.5, None, ALU.mult).then_inc(merge_steps, 1)
                        dve.wait_ge(merge_steps, i * (4 * RING) + (2 * n + 2))
                        vec.scalar_tensor_tensor(out=lo, in0=prod[2][:], scalar=0.5, in1=hi.bitcast(F32),
                                                 op0=ALU.mult, op1=ALU.subtract).then_inc(merged_ready, 1)
            with dve.Fori(0, KT // RING) as i:
                for j in range(RING):
                    for h in range(NH):
                        dve.wait_ge(msq_ready, i * (RING * NH) + (NH * j + h + 1))
                        vec.tensor_scalar(one(m, i * RING + j)[:, half_cols[h]], psum[:, h], 1.0, None, ALU.mult
                                          ).then_inc(m_ready, 1)
                        if h == 0:
                            split_lo(i * RING + (P_WO + j + 1), (j + 1) % RING)

            def inverse(n):
                dve.wait_ge(dev_ready, n + 1)
                vec.reciprocal(rstd[:], dev[:]).then_inc(rstd_ready, 1)
                dve.wait_ge(rstd_ready, n + 1)

            def scale_by(out_ap, in_ap, norm, kt, semaphore):
                col = PAR_G + norm * KT + kt
                vec.scalar_tensor_tensor(out=out_ap, in0=in_ap, scalar=par[:, col:col + 1], in1=rstd[:],
                                         op0=ALU.mult, op1=ALU.mult).then_inc(semaphore, 1)

            for h in range(NH):
                inverse(2 * h)
                if h == 0:
                    dve.wait_ge(m_ready, NH * KT + 2)
                for kt in range(KT):
                    scale_by(m[:, kt, half_cols[h]], m[:, kt, half_cols[h]], 1, kt, m_scaled)
                for kt in range(KT):
                    n = h * KT + kt
                    span = m[:, kt, half_cols[h]]
                    dve.wait_ge(m_scaled, n + 1)
                    dve.wait_ge(res_done, n + 1)
                    vec.tensor_tensor(span, psum[:, n % 4], span, ALU.add).then_inc(h_sum_ready, 1)
                inverse(2 * h + 1)
                dve.wait_ge(h_sum_ready, (h + 1) * KT)
                for kt in range(KT + 1):
                    n = h * KT + kt
                    if kt < KT:
                        wait(dve, u2_ready, n - 1)
                        scale_by(relu[n % 2][:], m[:, kt, half_cols[h]], 2, kt, u2_scaled)
                    if kt > 0:
                        dve.wait_ge(u2_hi, n)
                        lo_part(act_hl, (slice(None), kt - 1, half_cols[h]), relu[(n - 1) % 2][:], u2_ready)

            def chunk(i, last):
                for j in range(FF_PANELS):
                    if j < FFC:
                        for h in range(NH):
                            u = NH * j + h
                            if h == 0:
                                split_lo(i * FF_PANELS + (P_FF + j + 1), (j + 1) % RING)
                            dve.wait_ge(fsq_ready, i * FF1_UNITS + (u + 1))
                            vec.tensor_copy(f_hl[0][:, j, half_cols[h]], fsq[h][:]).then_inc(fhi_ready, 1)
                            dve.wait_ge(fhi_ready, i * FF1_UNITS + (u + 1))
                            lo_part(f_hl, (slice(None), j, half_cols[h]), fsq[h][:], f_ready)
                    else:
                        for dd in range(2):
                            for h in range(NH):
                                u = 4 * (j - FFC) + 2 * dd + h
                                dve.wait_ge(ff_done, i * FF_UNITS + (FF1_UNITS + u + 1))
                                dve.wait_ge(acc_done, i * FF2_UNITS + (u + 1))
                                span = acc[:, 2 * (j - FFC) + dd, half_cols[h]]
                                vec.tensor_tensor(span, psum[:, u % 4], span, ALU.add).then_inc(acc_done, 1)
                                if dd == 0 and h == 0 and not (last and j == FF_PANELS - 1):
                                    split_lo(i * FF_PANELS + (P_FF + j + 1), (j + 1) % RING)

            dve.wait_ge(acc_done, FF2_UNITS)
            with dve.Fori(0, CHUNKS - 1) as i:
                chunk(i, False)
            chunk(CHUNKS - 1, True)

            for h in range(NH):
                inverse(2 * NH + h)
                for kt in range(KT):
                    scale_by(acc[:, kt, half_cols[h]], acc[:, kt, half_cols[h]], 3, kt, y_scaled)
                for kt in range(KT):
                    dve.wait_ge(y_scaled, h * KT + kt + 1)
                    vec.tensor_tensor(m[:, kt, half_cols[h]], m[:, kt, half_cols[h]], acc[:, kt, half_cols[h]],
                                      ALU.add).then_inc(y_ready, 1)
            for t in range(TT):
                dve.wait_ge(yt_done, t + 1)
                wait(dve, stored[t % 2], 16 * (t // 2))
                vec.tensor_copy(ost[t % 2][:, HALF:D], psum[:, 2 * (t % 2) + 1]).then_inc(ost_ready[t % 2], 1)


NAMES = ["x", "w_in", "b_gate", "conv_w", "w_conv_out", "lambda_qk", "subln_g", "w_attn_out", "w_o", "norm_g",
         "w_ff1", "w_ff2"]


def kernel(**inputs):
    import numpy as np
    import concourse.bacc as bacc
    from concourse.bass_utils import run_bass_kernel_spmd

    nc = bacc.Bacc("TRN2", target_bir_lowering=False, num_devices=1)
    arrays, args = {}, []
    for name in NAMES:
        a = np.ascontiguousarray(inputs[name])
        arrays[f"in_{name}"] = a
        args.append(nc.dram_tensor(f"in_{name}", a.shape, mybir.dt.from_np(a.dtype), kind="ExternalInput").ap())
    args.append(nc.dram_tensor("out_0", (1, S, D), F32, kind="ExternalOutput").ap())
    build(nc, *args)
    r = run_bass_kernel_spmd(nc, [arrays], core_ids=[0])
    return r.results[0]["out_0"]
```

```python
from contextlib import ExitStack

import concourse.bass as bass
from concourse import mybir

ALU = mybir.AluOpType
ACT = mybir.ActivationFunctionType
F32 = mybir.dt.float32
F32R = mybir.dt.float32r

P = 128
D = 1024
S = 1024
KT = D // P
TT = S // P
HALF = 512
NH = S // HALF
CONV_K = 3
CT = D // 2 // P
HEADS = 4
HD = D // 16
QB = S // P
FF = 4 * D
FFC = 4
CHUNKS = FF // P // FFC
EPS = 1e-6
LAM_INIT = 0.8 - 0.6
SCALE = HD ** -0.5
SLOPES = [2.0 ** (-8.0 * (h + 1) / HEADS) for h in range(HEADS)]
RING = 2

PAR_G = 0
PAR_B = PAR_G + 4 * KT
PAR_C = PAR_B + 2 * KT
PAR_S = PAR_C + CONV_K * CT
NPAR = PAR_S + 1

COL_H, COL_B, COL_C = 0, CT * P, 2 * CT * P
COL_Q = 3 * CT * P
COL_K = COL_Q + HEADS * P
COL_V = COL_K + HEADS * P
COL_G = COL_V + HEADS * P


def steps(text):
    return [(word[:-1], int(word[-1])) for word in text.split()]


TURN = steps("C7 q0 O0 q1 T7 TL7 k0 AV1 k1 v0 O1 v1 S0 h0 VT0 X0 M0 C0 h1 S1 X1 T0 M1 TL0 C1 c0 S2 X2 T1 M2 "
             "TL1 C2 c1 S3 X3 b0 T2 M3 TL2 C3 b1 S4 X4 g0 T3 M4 TL3 C4 g1 AV0 S5 X5 T4 M5 TL4 C5 g2 S6 X6 T5 "
             "M6 TL5 C6 g3 S7 X7 T6 M7 TL6")
FROM_LAST_HEAD = steps("C7 O0 T7 TL7 AV1 O1")
FIRST_TURN = [x for x in TURN if x not in FROM_LAST_HEAD]
AFTER = [steps("C7 g0 O0 g1 T7 TL7 ZS0 g2 AV1 ZS1 g3 O1 ZS2"), steps("ZS3 OS0 g0 OS1 g1 OS2 g2 OS3 g3")]
PANELS = ["q", "k", "v", "h", "c", "b", "g"]
GATE_PANELS = 2
HEAD_PANELS = len(PANELS) - 1 + GATE_PANELS
HEAD_UNITS = 2 * HEAD_PANELS
GATE_TURNS = 2 * KT // GATE_PANELS
TB = {x: n for n, x in enumerate([x for x in FIRST_TURN if x[0] in ("VT", "T", "AV", "O")]
                                 + [x for x in FROM_LAST_HEAD if x[0] in ("T", "AV", "O")])}
TB_USES = len(TB)



def laced(units, side):
    return [x for n, unit in enumerate(units) for x in [unit] + side.get(n, [])]


def half_chunk(c, h):
    return [("F1", c, h, j) for j in range(FFC)] + [("F2", c, h, k) for k in range(KT)]


def panel_ends(items):
    return [x for x in items if x[0] in ("W", "F1") or x[0] == "F2" and x[3] % 2 == 1]


def mid_norms(h, per_unit, u_side):
    side = {n: [] for n in range(KT)}
    side[0] = [("MS", h)]
    side[1] = [("B", 2 * h)]
    for k in range(KT):
        side[1 + k // per_unit].append(("R", h, k))
    for k in range(KT):
        side[2 + k // per_unit].insert(k % per_unit, ("Q", h, k))
    last = 2 + (KT - 1) // per_unit
    side[last].append(("HS", h))
    side[last + 1] = [("B", 2 * h + 1)]
    k = 0
    for n, tiles in enumerate(u_side):
        side.setdefault(last + 1 + n, []).extend(("U", h, j) for j in range(k, k + tiles))
        k += tiles
    return side


MIDDLE = (laced([("W", n) for n in range(KT)], mid_norms(0, 4, (3, 3, 2)))
          + laced(half_chunk(0, 0), mid_norms(1, 3, (2, 2, 2, 2))) + half_chunk(0, 1))
TILES_HALF = TT // NH
LAST = CHUNKS - 1

def end_norms():
    side = {n: [] for n in range(FFC + KT)}
    for n in range(3):
        side[n] += [("YQ", 0, k) for k in range(4 * n - 4, 4 * n) if k >= 0]
        side[n] += [("YS", 0, k) for k in range(4 * n, 4 * n + 4) if k < KT]
    side[2] += [("YN", 0)]
    side[3] += [("B", 2 * NH)]
    for k in range(KT):
        side[3 + k // 2].append(("Y", 0, k))
        side[FFC + k] += ([("YQ", 1, k - 1)] if k > 0 else []) + [("YS", 1, k)]
    for t in range(TILES_HALF):
        side[(8, 9, 10, 11)[t]].append(("YT", 0, t))
    return side


END = (half_chunk(LAST, 0) + laced(half_chunk(LAST, 1), end_norms()) + [("YQ", 1, KT - 1), ("YN", 1), ("B", 2 * NH + 1)]
       + [("Y", 1, k) for k in range(KT)])
FF_BANKS = (0, 1, 6, 7)
RES_BANKS = ((2, 3, 5, 6), (2, 3, 5))
SUM_BANK = 4

PASSES = ((0, 0), (0, 1), (1, 0))


def unit_of(i, kind, n, after=False):
    if after:
        return i * (2 * GATE_PANELS) + (2 * HEADS * (len(PANELS) - 1) + n)
    return i * HEAD_UNITS + (2 * PANELS.index(kind) + n)


def panel_of(i, kind, n, after=False, ahead=0):
    per, first = (GATE_PANELS, HEADS * (len(PANELS) - 1)) if after else (HEAD_PANELS, PANELS.index(kind))
    j = first + n // 2 + ahead
    return i * per + j, j % RING, i * (per // RING) + j // RING


def tb_use(i, kind, n):
    return (i - ((kind, n) in FROM_LAST_HEAD)) * TB_USES + TB[kind, n]


def one(ap, i):
    return ap[:, bass.ds(i, 1)].rearrange("p o c -> p (o c)")


def build(nc, x, w_in, b_gate, conv_w, w_conv_out, lambda_qk, subln_g, w_attn_out, w_o, norm_g,
          w_ff1, w_ff2, out):
    ctx = ExitStack()

    def sb(name, shape, dt=F32, scope=None):
        return (scope or ctx).enter_context(nc.sbuf_tensor(name, shape, dt))

    def sem(name):
        return ctx.enter_context(nc.semaphore(name))

    with ctx:
        act_hl = [sb("act_hi", [P, KT, S], F32R), sb("act_lo", [P, KT, S], F32R)]
        w_raw = [sb(f"w_raw{s}", [P, KT, P]) for s in range(RING)]
        w_hl = [[sb(f"w_hi{s}", [P, KT, P], F32R), sb(f"w_lo{s}", [P, KT, P], F32R)] for s in range(RING)]
        ident = sb("ident", [P, P])
        ones = sb("ones", [P, P])
        par = sb("par", [P, NPAR + 2])
        gate_bias = sb("gate_bias", [P, GATE_PANELS])
        stats = sb("stats", [P, 2 * TT])
        small = sb("small", [P, 28])
        staging = [sb(f"staging{s}", [P, HALF]) for s in range(2)]
        dev = sb("dev", [P, HALF])
        neg_lam = par[:, NPAR:NPAR + 1]
        sub_gain = par[:, NPAR + 1:NPAR + 2]
        neg_max, exp_sum, recip = small[:, 0:2], small[:, 2:4], small[:, 4:6]
        weight2, eps, spare, maxima = small[:, 6:7], small[:, 7:8], small[:, 8:9], small[:, 10:12]
        tok_dev, tok_inv = small[:, 20:24], small[:, 24:28]
        dots, dot_exp, lam_diff = small[:, 12:14], small[:, 14:16], small[:, 16:17]

        with ExitStack() as scope:
            z = sb("z", [P, CT, S], scope=scope)
            o = sb("o", [P, HEADS, S], scope=scope)
            with ExitStack() as loop_scope:
                table = sb("alibi", [P, 2 * S - P], scope=loop_scope)
                inner = sb("inner", [P, S + 2], scope=loop_scope)
                with ExitStack() as s1:
                    xn = sb("xn", [P, TT, D], scope=s1)
                    xsq = [sb(f"xsq{s}", [P, D], scope=s1) for s in range(2)]
                    par_rows = sb("par_rows", [NPAR, P], scope=s1)
                    lqk = sb("lqk", [P, 4, HD], scope=s1)
                    lq_junk = sb("lq_junk", [P, HD], scope=s1)
                with ExitStack() as s2:
                    q_st = [sb(f"q_stack{c}", [P, S], F32R, s2) for c in range(2)]
                    k_st = [sb(f"k_stack{c}", [P, S], F32R, s2) for c in range(2)]
                    k_lo = sb("k_lo", [P, S], F32R, s2)
                    v_hl = [sb("v_hi", [P, TT, P], F32R, s2), sb("v_lo", [P, TT, P], F32R, s2)]
                    e = [sb(f"e{c}", [P, S], scope=s2) for c in range(2)]
                    vt = e[1]
                    at_hl = [sb("at_hi", [P, TT, HALF], F32R, s2), sb("at_lo", [P, TT, HALF], F32R, s2)]
            with ExitStack() as s3:
                z_hl = [sb("z_hi", [P, CT, S], F32R, s3), sb("z_lo", [P, CT, S], F32R, s3)]
                o_hl = [sb("o_hi", [P, HEADS, S], F32R, s3), sb("o_lo", [P, HEADS, S], F32R, s3)]
                gate_in = [sb(f"gate_in{s}", [P, 2, HALF], scope=s3) for s in range(2)]
                prod = [sb(f"prod{s}", [P, HALF], scope=s3) for s in range(3)]
        m = sb("m", [P, KT, S])
        with ExitStack() as s4:
            x2 = sb("x2", [P, TT, D], scope=s4)
        acc = sb("acc", [P, NH, KT, HALF])
        relu = [sb(f"relu{s}", [P, HALF]) for s in range(2)]
        sq = [sb(f"sq{s}", [P, HALF]) for s in range(2)] + staging
        rstd = sb("rstd", [P, HALF])
        with ExitStack() as s5:
            ssq = [sb(f"ssq{s}", [P, HALF], scope=s5) for s in range(NH)]
        ost0 = sb("ost0", [P, D])
        with ExitStack() as s6:
            f_hl = [sb("f_hi", [P, FFC, S], F32R, s6), sb("f_lo", [P, FFC, S], F32R, s6)]
        ost1 = [sb(f"ost1_{t}", [P, D]) for t in range(TILES_HALF)]

        psum = ctx.enter_context(nc.psum_tensor("psum", [P, 8, HALF], F32))
        SB, TBK = 2, 6
        gates = nc.dram_tensor("gates_scratch", [2, KT, P, S], F32, kind="Internal").ap()

        x_landed = [sem(f"x_landed{t}") for t in range(TT)]
        par_landed = sem("par_landed")
        lqk_landed = sem("lambda_qk_landed")
        setup = sem("setup")
        vec_setup = sem("vector_setup")
        par_t = sem("par_transposed")
        par_ready = sem("par_ready")
        dots_ready = sem("lambda_dots_ready")
        dot_exp_ready = sem("lambda_exp_ready")
        row_sums = [sem(f"row_sums{s}") for s in range(2)]
        row_dev = sem("row_deviations")
        row_rstd = sem("row_rstd")
        xn_ready = sem("x_normed")
        xt_done = sem("x_transposed")
        u_hi = sem("u_hi")
        u_ready = sem("u_ready")
        w_landed = [sem(f"w_landed{s}") for s in range(RING)]
        w_hi = sem("w_hi_ready")
        w_split = sem("w_split")
        proj_done = sem("proj_done")
        qk_hi = sem("qk_hi")
        qk_ready = sem("qk_ready")
        vt_ready = sem("vt_ready")
        h_ready = sem("h_ready")
        c_ready = sem("c_times_h_ready")
        taps = sem("conv_taps")
        z_ready = sem("z_ready")
        bias_ready = sem("gate_bias_ready")
        gate_ready = sem("gate_ready")
        gate_stored = [sem(f"gate_stored{s}") for s in range(2)]
        tb_done = sem("tb_done")
        tb_hi = sem("tb_hi")
        tb_free = sem("tb_free")
        s_done = sem("scores_done")
        s_read = sem("scores_read")
        map1_read = sem("map1_read")
        table_ready = sem("alibi_scaled")
        max_ready = sem("max_ready")
        exp_done = sem("exp_done")
        combine = sem("combine_steps")
        a_ready = sem("a_ready")
        zhi_ready = sem("z_hi_ready")
        zlo_ready = sem("z_lo_ready")
        osq_ready = sem("o_squares_ready")
        orstd_ready = sem("o_inverses_ready")
        o_scaled = sem("o_scaled")
        ohi_ready = sem("o_hi_ready")
        olo_ready = sem("o_lo_ready")
        gate_landed = [sem(f"gate_landed{s}") for s in range(2)]
        br_done = sem("branches_done")
        br_read = sem("branches_read")
        merge_steps = sem("merge_steps")
        merged_ready = sem("merged_ready")
        wo_done = sem("wo_done")
        m_ready = sem("m_ready")
        msq_ready = sem("m_squares_ready")
        msq_added = sem("m_squares_added")
        x2_landed = sem("x2_landed")
        msum_done = sem("m_sums_done")
        dev_ready = sem("deviations_ready")
        inv_ready = sem("inverses_ready")
        diag_ready = sem("inverses_on_diagonals")
        spread_done = sem("inverses_spread")
        rstd_ready = sem("rstd_ready")
        res_done = sem("residual_transposed")
        m_scaled = sem("m_scaled")
        h_sum_ready = sem("residual_added")
        sq_ready = sem("squares_ready")
        sq_summed = sem("squares_summed")
        u2_scaled = sem("u2_scaled")
        u2_hi = sem("u2_hi")
        u2_ready = sem("u2_ready")
        ff_done = sem("ff_done")
        relu_done = sem("relu_done")
        relu_squared = sem("relu_squared")
        fhi_ready = sem("f_hi_ready")
        f_ready = sem("f_ready")
        acc_done = sem("acc_done")
        y_scaled = sem("y_scaled")
        y_ready = [sem("y_by_vector"), sem("y_by_pool")]
        yt_done = [sem(f"y_transposed{h}") for h in range(NH)]
        ost0_ready = sem("ost0_ready")
        stored0 = sem("stored0")
        ost1_act, ost1_vec = sem("ost1_by_activation"), sem("ost1_by_vector")
        stored1 = sem("stored1")

        x_tiles = x.rearrange("b (t p) d -> p (b t) d", p=P)
        out_tiles = out.rearrange("b (t p) d -> p (b t) d", p=P)
        w_in_t, w_co_t, w_ao_t, w_o_t, w1_t, w2_t = (
            w.rearrange("l (k p) n -> p (l k) n", p=P) for w in (w_in, w_conv_out, w_attn_out, w_o, w_ff1, w_ff2))

        P_BR = HEADS * (len(PANELS) - 1) + 2 * KT
        P_WO = P_BR + KT
        P_FF = P_WO + NH * KT
        FF_PANELS = FFC + KT // 2
        P_LOOP = P_FF + (NH - 1) * FF_PANELS
        P_END = P_LOOP + (LAST + NH) * FF_PANELS
        GATE_UNITS = 2 * GATE_PANELS
        FF1_UNITS, FF2_UNITS = NH * FFC, NH * KT
        FF_UNITS = FF1_UNITS + FF2_UNITS
        BANKS = len(FF_BANKS)
        tb_tiles = psum[:, TBK:TBK + 2].rearrange("p b (k c) -> p (b k) c", c=P)
        own = [slice(c * HD, (c + 1) * HD) for c in range(2)]
        other = [own[1], own[0]]
        half_cols = [slice(h * HALF, (h + 1) * HALF) for h in range(NH)]

        def wait(eng, semaphore, value):
            if not isinstance(value, int) or value > 0:
                eng.wait_ge(semaphore, value)

        def y_adder(h, kt):
            return (1, kt + 1) if h == 0 else (kt % 2, (kt // 2 + 1) + (kt % 2) * KT)

        def ff_panel(c, h, kind, n):
            return (P_FF if c == 0 else P_LOOP + LAST * FF_PANELS) + h * FF_PANELS + (n if kind == "F1" else FFC + n // 2)

        block = ctx.enter_context(nc.Block())

        @block.sync
        def _(sp):
            def load(panel, slot, *pairs):
                wait(sp, w_split, panel - (RING - 1))
                for dst, src in pairs:
                    sp.dma_start(dst, src).then_inc(w_landed[slot], 32 // len(pairs))

            def w_in_panel(panel, slot, column):
                load(panel, slot, (w_raw[slot][:], w_in_t.rearrange("p k (b c) -> p k b c", c=P)
                                   [:, :, bass.ds(column, 1)].rearrange("p k b c -> p k (b c)")))

            def head_panels(i, js):
                columns = [i + col // P for col in (COL_Q, COL_K, COL_V, COL_H, COL_C, COL_B)]
                columns += [i * GATE_PANELS + (COL_G // P + g) for g in range(GATE_PANELS)]
                for j in js:
                    w_in_panel(i * HEAD_PANELS + j, j % RING, columns[j])

            for h in range(NH):
                for t in range(h * TT // NH, (h + 1) * TT // NH):
                    sp.dma_start(xn[:, t], x_tiles[:, t]).then_inc(x_landed[t], 16)
                head_panels(0, [h])
            head_panels(0, range(NH, HEAD_PANELS))
            with sp.Fori(1, HEADS) as i:
                head_panels(i, range(HEAD_PANELS))
            with sp.Fori(HEADS, GATE_TURNS) as i:
                for g in range(GATE_PANELS):
                    w_in_panel(i * GATE_PANELS + (P_BR - 2 * KT + g), g % RING, i * GATE_PANELS + (COL_G // P + g))
            def branch_load(i, j, panel):
                cols = bass.ds(i * (RING * P) + j * P, P)
                load(panel, j, (w_raw[j][:, 0:CT], w_co_t[:, :, cols]), (w_raw[j][:, CT:KT], w_ao_t[:, :, cols]))

            def w_o_load(i, j, panel):
                load(panel, j, (w_raw[j][:], w_o_t[:, :, bass.ds(i * (RING * P) + j * P, P)]))

            def branch_turn(i, next_load):
                for j in range(RING):
                    next_load(j)
                    for h in range(NH):
                        if isinstance(i, int):
                            sp.wait_ge(gate_stored[h], 16 * (KT + i * RING + j + 1))
                        sp.wait_ge(br_read, i * (4 * RING) + 4 * j + 2 * h + 2)
                        sp.dma_start(gate_in[h][:], gates[:, bass.ds(i * RING + j, 1), :, half_cols[h]]
                                     .rearrange("b o p c -> p (b o) c")).then_inc(gate_landed[h], 16)

            for j in range(RING):
                branch_load(0, j, P_BR + j)
            branch_turn(0, lambda j: branch_load(1, j, P_BR + RING + j))
            for h in range(NH):
                sp.wait_ge(gate_stored[h], 16 * 2 * KT)
            with sp.Fori(1, KT // RING - 1) as i:
                branch_turn(i, lambda j: branch_load(i + 1, j, i * RING + (P_BR + RING + j)))
            branch_turn(KT // RING - 1, lambda j: w_o_load(0, j, P_WO + j))
            sp.wait_ge(br_done, 4 * KT)
            for j in range(RING):
                sp.dma_start(x2[:, j], x_tiles[:, j]).then_inc(x2_landed, 16)
            with sp.Fori(1, KT // RING) as i:
                for j in range(RING):
                    w_o_load(i, j, i * RING + (P_WO + j))
                    sp.dma_start(x2[:, bass.ds(i * RING + j, 1)], x_tiles[:, bass.ds(i * RING + j, 1)]
                                 ).then_inc(x2_landed, 16)
            with sp.Fori(0, KT // RING) as i:
                for j in range(RING):
                    w_o_load(i, j, i * RING + (P_WO + KT + j))

            def ff_panels(c, first):
                for j in range(FFC):
                    load(first + j, j % RING, (w_raw[j % RING][:], w1_t[:, :, bass.ds(c * (FFC * P) + j * P, P)]))
                for j in range(KT // 2):
                    slot = (FFC + j) % RING
                    load(first + (FFC + j), slot,
                         (w_raw[slot][:].rearrange("p (k d) c -> p k (d c)", d=2),
                          w2_t[:, bass.ds(c * FFC, FFC), j * 2 * P:(j + 1) * 2 * P]))

            for h in range(NH):
                ff_panels(0, ff_panel(0, h, "F1", 0))
            with sp.Fori(1, LAST) as i:
                ff_panels(i, i * FF_PANELS + P_LOOP)
            for h in range(NH):
                ff_panels(LAST, ff_panel(LAST, h, "F1", 0))
            for b in range(2):
                for t in range(TILES_HALF):
                    if b == 0:
                        sp.wait_ge(ost1_act, t + 1)
                    else:
                        sp.wait_ge((ost1_act, ost1_vec)[t % 2], (TILES_HALF, 0)[t % 2] + t // 2 + 1)
                    sp.dma_start(out_tiles[:, TILES_HALF + t, half_cols[b]], ost1[t][:, half_cols[b]]
                                 ).then_inc(stored1, 16)
            sp.wait_ge(stored0, 16 * TILES_HALF)
            sp.wait_ge(stored1, 16 * 2 * TILES_HALF)

        @block.gpsimd
        def _(pool):
            nc.gpsimd.memset(ident[:], 1.0).then_inc(setup, 1)
            pool.wait_ge(setup, 1)
            nc.gpsimd.affine_select(out=ident[:], in_=ident[:], compare_op=ALU.is_equal, fill=0.0, base=0,
                                    pattern=[[-1, P]], channel_multiplier=1).then_inc(setup, 1)
            nc.gpsimd.memset(ones[:], 1.0).then_inc(setup, 1)
            nc.gpsimd.iota(table[:], [[-1, 2 * S - P]], base=S - P, channel_multiplier=1,
                           allow_small_or_imprecise_dtypes=True).then_inc(setup, 1)
            nc.gpsimd.memset(inner[:], 0.0).then_inc(setup, 1)
            pool.wait_ge(wo_done, 1)
            for h in range(NH):
                nc.gpsimd.memset(ssq[h][:], 0.0).then_inc(msq_added, 1)
            pool.wait_ge(msq_added, NH)

            def add_squares(number, slot, h):
                pool.wait_ge(msq_ready, number + 1)
                pool.wait_ge(msq_added, number + 2)
                nc.gpsimd.tensor_tensor(ssq[h][:], ssq[h][:], relu[slot][:], ALU.add).then_inc(msq_added, 1)

            with pool.Fori(0, KT // RING) as i:
                for j in range(RING):
                    add_squares(i * RING + j, j, 0)
            pool.wait_ge(w_split, P_WO + KT + RING)
            for panel, item in enumerate(panel_ends(MIDDLE), P_WO + KT):
                slot, nxt = panel % RING, panel + RING
                pool.wait_ge(w_hi, nxt + 1)
                nc.gpsimd.tensor_tensor(w_hl[slot][1][:], w_raw[slot][:], w_hl[slot][0][:].bitcast(F32), ALU.subtract
                                        ).then_inc(w_split, 1)
                if item[0] == "W":
                    add_squares(KT + item[1], item[1] % RING, 1)
            for kind, *where in END:
                if kind == "Y" and y_adder(*where)[0] == 1:
                    h, kt = where
                    pool.wait_ge(y_scaled, h * KT + kt + 1)
                    span = m[:, kt, half_cols[h]]
                    nc.gpsimd.tensor_tensor(span, span, acc[:, h, kt], ALU.add).then_inc(y_ready[1], 1)
                elif kind == "YT":
                    _, t = where
                    pool.wait_ge(ost0_ready, 2 * (t + 1))
                    nc.gpsimd.dma_start(out_tiles[:, t], ost0[:]).then_inc(stored0, 16)

        @block.tensor
        def _(pe):
            pe.sem_inc(m_ready, 2)

            def product(bank, stat, moving, kts, last=None, between=()):
                sums = list(between)
                per_kt = -(-len(sums) // (len(kts) - 1))
                terms = [(kt, a, b) for kt in kts for a, b in PASSES]
                for t, (kt, a, b) in enumerate(terms):
                    if last and t == len(terms) - len(PASSES):
                        pe.wait_ge(*last)
                    mm = nc.tensor.matmul(bank, stat(a, kt), moving(b, kt), start=(t == 0),
                                          stop=(t == len(terms) - 1))
                    if (a, b) == PASSES[-1]:
                        for _ in range(min(per_kt, len(sums))):
                            square_sum(sums.pop(0))
                return mm

            pe.wait_ge(par_landed, 16 * 4)
            pe.wait_ge(setup, 3)
            nc.tensor.transpose(psum[:, 7, 0:NPAR], par_rows[:], ident[0:NPAR, 0:NPAR]).then_inc(par_t, 1)

            def turn_x(h):
                pe.wait_ge(xn_ready, (h + 1) * (TT // NH))
                for kt in range(KT):
                    n = h * KT + kt
                    wait(pe, u_ready, n - 3)
                    for t in range(4):
                        mm = nc.tensor.transpose(psum[:, SB + n % 4, t * P:(t + 1) * P],
                                                 xn[:, 4 * h + t, kt * P:(kt + 1) * P], ident[:])
                    mm.then_inc(xt_done, 1)

            def walk(i, steps, after=False):
                for kind, n in steps:
                    if kind in PANELS:
                        h = n % NH
                        panel, slot, _ = panel_of(i, kind, n, after)
                        if h == 0:
                            pe.wait_ge(w_split, panel + 1)
                        if kind == "q":
                            wait(pe, gate_ready, i * GATE_UNITS - (1 - h))
                        elif kind == "k":
                            pe.wait_ge(qk_ready, i * 4 + (1 + h))
                        elif kind == "v":
                            pe.wait_ge(qk_ready, i * 4 + (3 + h))
                        elif kind == "h":
                            pe.wait_ge(vt_ready, i * 2 + (1 + h))
                        elif kind == "c":
                            pe.wait_ge(h_ready, i * 2 + (1 + h))
                        elif kind == "b":
                            pe.wait_ge(c_ready, i * 2 + (1 + h))
                        elif n < 2 and not after:
                            pe.wait_ge(z_ready, i * 2 + (1 + h))
                        else:
                            pe.wait_ge(gate_ready, i * GATE_UNITS + (n - 1))
                        product(psum[:, h], lambda a, kt: w_hl[slot][a][:, kt],
                                lambda b, kt: act_hl[b][:, kt, half_cols[h]], range(KT)).then_inc(proj_done, 1)
                    elif kind == "S":
                        if n == 0:
                            pe.wait_ge(qk_ready, i * 4 + 4)
                        wait(pe, s_read, i * QB + n)
                        for c in range(2):
                            for half in range(NH):
                                nc.tensor.matmul(psum[:, SB + 2 * c + half], q_st[c][:, n * P:(n + 1) * P],
                                                 k_st[c][:, half_cols[half]], start=True, stop=False)
                        for half in range(NH):
                            for c in range(2):
                                mm = nc.tensor.matmul(psum[:, SB + 2 * c + half], q_st[c][own[c], n * P:(n + 1) * P],
                                                      k_lo[own[c], half_cols[half]], start=False, stop=True)
                        mm.then_inc(s_done, 1)
                    elif kind in ("VT", "T"):
                        if kind == "VT":
                            pe.wait_ge(vt_ready, i * 2 + 2)
                        else:
                            pe.wait_ge(a_ready, i * QB + (n + 1 if n < 7 else 0))
                        wait(pe, tb_free, tb_use(i, kind, n))
                        src = vt if kind == "VT" else e[0]
                        for k in range(TT):
                            mm = nc.tensor.transpose(psum[:, TBK + k // 4, (k % 4) * P:(k % 4 + 1) * P],
                                                     src[:, k * P:(k + 1) * P], ident[:])
                        mm.then_inc(tb_done, 1)
                    elif kind == "AV":
                        pe.wait_ge(tb_free, tb_use(i, kind, n))
                        product(psum[:, TBK], lambda a, kt: v_hl[a][:, kt], lambda b, kt: at_hl[b][:, kt],
                                range(TT)).then_inc(tb_done, 1)
                    elif kind == "O":
                        pe.wait_ge(osq_ready, i * 2 + (n - 1))
                        pe.wait_ge(tb_free, tb_use(i, kind, n))
                        nc.tensor.matmul(psum[:, TBK], ones[:], dev[:], start=True, stop=True).then_inc(tb_done, 1)

            turn_x(0)
            pe.wait_ge(u_ready, KT)
            walk(0, FIRST_TURN[:1])
            turn_x(1)
            pe.wait_ge(u_ready, NH * KT)
            walk(0, FIRST_TURN[1:])
            with pe.Fori(1, HEADS) as i:
                walk(i, TURN)
            walk(HEADS, AFTER[0], True)
            walk(HEADS + 1, AFTER[1], True)
            pe.wait_ge(s_read, HEADS * QB)
            pe.wait_ge(tb_free, HEADS * TB_USES)
            pe.sem_inc(br_read, 4)
            with pe.Fori(HEADS + len(AFTER), GATE_TURNS) as i:
                walk(i, [("g", n) for n in range(GATE_UNITS)], True)

            pe.wait_ge(gate_ready, GATE_TURNS * GATE_UNITS)
            pe.wait_ge(zlo_ready, CT)
            pe.wait_ge(olo_ready, HEADS)
            with pe.Fori(0, KT // RING) as i:
                for j in range(RING):
                    pe.wait_ge(w_split, i * RING + (P_BR + j + 1))
                    for h in range(NH):
                        for br in range(2):
                            pe.wait_ge(br_read, i * (4 * RING) + (4 * j + 2 * h + br + 1))
                            src = (z_hl, o_hl)[br]
                            product(psum[:, 2 * h + br], lambda a, kt: w_hl[j][a][:, CT * br + kt],
                                    lambda b, kt: src[b][:, kt, half_cols[h]], range(CT)).then_inc(br_done, 1)

            pe.wait_ge(br_read, 4 * KT + 2)
            pe.wait_ge(merged_ready, NH * KT - 1)

            def w_o_unit(slot, panel, number, h, between=()):
                pe.wait_ge(w_split, panel + 1)
                pe.wait_ge(m_ready, number + 1)
                product(psum[:, slot], lambda a, kt: w_hl[slot][a][:, kt],
                        lambda b, kt: act_hl[b][:, kt, half_cols[h]], range(KT), between=between
                        ).then_inc(wo_done, 1)

            with pe.Fori(0, KT // RING) as i:
                for j in range(RING):
                    w_o_unit(j, i * RING + (P_WO + j), i * RING + j, 0)

            def ff1_unit(bank, slot, h, between=()):
                product(psum[:, bank], lambda a, kt: w_hl[slot][a][:, kt],
                        lambda b, kt: act_hl[b][:, kt, half_cols[h]], range(KT), between=between
                        ).then_inc(ff_done, 1)

            def ff2_unit(bank, slot, dd, h, last=None, between=()):
                product(psum[:, bank], lambda a, kt: w_hl[slot][a][:, 2 * kt + dd],
                        lambda b, kt: f_hl[b][:, kt, half_cols[h]], range(FFC), last, between
                        ).then_inc(ff_done, 1)

            def token_sums(src, first, last):
                for t in range(TILES_HALF):
                    mm = nc.tensor.matmul(psum[:, SUM_BANK, t:t + 1], src[:, t * P:(t + 1) * P], ones[:, 0:1],
                                          start=(first and t == 0), stop=(last and t == TILES_HALF - 1),
                                          skip_group_check=True)
                return mm

            def square_sum(n):
                if n % KT == 0:
                    pe.wait_ge(rstd_ready, 2 * (n // KT) + 1 if n < NH * KT else NH + n // KT)
                pe.wait_ge(sq_ready, n + 1)
                token_sums(sq[n % 4], n % KT == 0, n % KT == KT - 1).then_inc(sq_summed, 1)

            def walk2(items):
                sums = []
                for kind, *where in items:
                    if kind in ("MS", "B", "Y"):
                        for n in sums:
                            square_sum(n)
                        sums = []
                    if kind == "W":
                        n, = where
                        if n == 0:
                            pe.wait_ge(merged_ready, NH * KT)
                        w_o_unit(n % RING, P_WO + KT + n, KT + n, 1, sums)
                    elif kind == "MS":
                        h, = where
                        pe.wait_ge(msq_added, NH + KT * (h + 1))
                        wait(pe, rstd_ready, 2 * h)
                        token_sums(ssq[h], True, True).then_inc(msum_done, 1)
                    elif kind == "B":
                        n, = where
                        pe.wait_ge(diag_ready, n + 1)
                        nc.tensor.matmul(psum[:, SUM_BANK], ones[:], dev[:], start=True, stop=True
                                         ).then_inc(spread_done, 1)
                    elif kind == "R":
                        h, kt = where
                        banks = RES_BANKS[h]
                        if h + kt == 0:
                            pe.wait_ge(x2_landed, 16 * TT)
                        wait(pe, h_sum_ready, h * KT + max(kt + 1 - len(banks), 0))
                        for t in range(4):
                            mm = nc.tensor.transpose(psum[:, banks[kt % len(banks)], t * P:(t + 1) * P],
                                                     x2[:, 4 * h + t, kt * P:(kt + 1) * P], ident[:])
                        mm.then_inc(res_done, 1)
                    elif kind == "Q":
                        h, kt = where
                        sums.append(h * KT + kt)
                    elif kind == "F1":
                        c, h, j = where
                        panel = ff_panel(c, h, "F1", j)
                        pe.wait_ge(w_split, panel + 1)
                        if c + h == 0:
                            if j < NH:
                                pe.wait_ge(m_ready, 2 + NH * KT - 1 + j)
                        else:
                            pe.wait_ge(acc_done, c * FF2_UNITS + h * KT - BANKS + j + 1)
                        if c == 0 and j == 0:
                            pe.wait_ge(u2_ready, (h + 1) * KT)
                        ff1_unit(FF_BANKS[j % BANKS], panel % RING, h, sums)
                    elif kind == "F2":
                        c, h, k = where
                        panel = ff_panel(c, h, "F2", k)
                        if k % 2 == 0:
                            pe.wait_ge(w_split, panel + 1)
                        last = None
                        if k == 0:
                            pe.wait_ge(f_ready, c * FF1_UNITS + (h + 1) * FFC - 1)
                            last = (f_ready, c * FF1_UNITS + (h + 1) * FFC)
                        if k < BANKS:
                            pe.wait_ge(relu_done, c * FF1_UNITS + h * FFC + k + 1)
                        else:
                            pe.wait_ge(acc_done, c * FF2_UNITS + h * KT + k - BANKS + 1)
                        ff2_unit(FF_BANKS[k % BANKS], panel % RING, k % 2, h, last, sums)
                    elif kind == "YQ":
                        h, kt = where
                        sums.append((NH + h) * KT + kt)
                    elif kind == "YT":
                        _, t = where
                        pe.wait_ge(y_ready[1], KT)
                        wait(pe, ost0_ready, 2 * t)
                        for kt in range(KT):
                            mm = nc.tensor.transpose(psum[:, 2 + kt // 4, (kt % 4) * P:(kt % 4 + 1) * P],
                                                     m[:, kt, t * P:(t + 1) * P], ident[:])
                        mm.then_inc(yt_done[0], 1)
                    elif kind == "Y" and where[0] == 1:
                        _, kt = where
                        if kt == 0:
                            pe.wait_ge(acc_done, CHUNKS * FF2_UNITS)
                            pe.wait_ge(ost0_ready, 2 * TILES_HALF)
                            pe.wait_ge(rstd_ready, 3 * NH)
                        adder, count = y_adder(1, kt)
                        pe.wait_ge(y_ready[adder], count)
                        for t in range(TILES_HALF):
                            mm = nc.tensor.transpose(psum[:, 2 * t + kt // 4, (kt % 4) * P:(kt % 4 + 1) * P],
                                                     m[:, kt, HALF + t * P:HALF + (t + 1) * P], ident[:])
                        mm.then_inc(yt_done[1], 1)
                    if kind in ("W", "F1", "F2"):
                        sums = []

            walk2(MIDDLE)
            with pe.Fori(1, LAST) as i:
                for j in range(FFC):
                    pe.wait_ge(w_split, i * FF_PANELS + (P_LOOP + j + 1))
                    for h in range(NH):
                        u = NH * j + h
                        if u < BANKS:
                            pe.wait_ge(acc_done, i * FF2_UNITS - BANKS + u + 1)
                        else:
                            pe.wait_ge(relu_done, i * FF1_UNITS + (u - BANKS + 1))
                        ff1_unit(FF_BANKS[u % BANKS], j % RING, h)
                for j in range(KT // 2):
                    pe.wait_ge(w_split, i * FF_PANELS + (P_LOOP + FFC + j + 1))
                    for dd in range(2):
                        for h in range(NH):
                            u = 4 * j + 2 * dd + h
                            if u < NH:
                                pe.wait_ge(f_ready, i * FF1_UNITS + (FF1_UNITS - 1 + h))
                            if u < BANKS:
                                pe.wait_ge(relu_done, i * FF1_UNITS + (FF1_UNITS - BANKS + u + 1))
                            else:
                                pe.wait_ge(acc_done, i * FF2_UNITS + (u - BANKS + 1))
                            ff2_unit(FF_BANKS[u % BANKS], (FFC + j) % RING, dd, h)
            walk2(END)

        @block.scalar
        def _(act):
            for src, a, b in ((norm_g, PAR_G, PAR_B), (b_gate, PAR_B, PAR_C), (conv_w, PAR_C, PAR_S)):
                act.dma_start(par_rows[a:b, :], src.rearrange("l n (k c) -> (l n k) c", c=P)).then_inc(par_landed, 16)
            act.dma_start(par_rows[PAR_S:NPAR, :], subln_g).then_inc(par_landed, 16)
            act.dma_start(lqk[:].rearrange("p n c -> p (n c)"),
                          lambda_qk.rearrange("l n c -> l (n c)").to_broadcast([P, 4 * HD])).then_inc(lqk_landed, 16)
            nc.scalar.preload_act_table(ACT.Sqrt)

            def split_hi(panel, slot, turns):
                act.wait_ge(w_landed[slot], turns * 32 + 32)
                nc.scalar.activation(w_hl[slot][0][:], w_raw[slot][:], ACT.Copy).then_inc(w_hi, 1)

            def squares(n, src):
                if n == 0:
                    for s in range(2):
                        act.wait_ge(gate_stored[s], 16 * 2 * KT)
                if n % KT == 0:
                    wait(act, u2_ready, min(n, NH * KT))
                wait(act, sq_summed, n - 3)
                nc.scalar.activation(sq[n % 4][:], src, ACT.Square).then_inc(sq_ready, 1)

            def row_sum(t):
                act.wait_ge(x_landed[t], 16)
                wait(act, row_sums[0], t // 2)
                nc.scalar.activation(xsq[0][:], xn[:, t], ACT.Square, accum_out=stats[:, t:t + 1]
                                     ).then_inc(row_sums[0], 1)

            def row_deviations(h):
                for s in range(2):
                    act.wait_ge(row_sums[s], 2 * h + 2)
                nc.scalar.activation(stats[:, TT + 4 * h:TT + 4 * h + 4], stats[:, 4 * h:4 * h + 4], ACT.Sqrt,
                                     bias=eps, scale=1.0 / D).then_inc(row_dev, 1)

            def u_hi_parts(h):
                for kt in range(KT):
                    n = h * KT + kt
                    act.wait_ge(xt_done, n + 1)
                    nc.scalar.activation(act_hl[0][:, kt, half_cols[h]], psum[:, SB + n % 4], ACT.Copy,
                                         scale=par[:, PAR_G + kt:PAR_G + kt + 1]).then_inc(u_hi, 1)

            row_sum(0)
            row_sum(2)
            act.wait_ge(vec_setup, 1)
            row_deviations(0)
            split_hi(0, 0, 0)
            row_sum(4)
            act.wait_ge(par_ready, 1)
            u_hi_parts(0)
            row_sum(6)
            row_deviations(1)
            u_hi_parts(1)
            split_hi(1, 1, 0)
            nc.scalar.preload_act_table(ACT.Exp)
            act.wait_ge(dots_ready, 2)
            nc.scalar.activation(dot_exp, dots, ACT.Exp).then_inc(dot_exp_ready, 1)

            def walk(i, steps, after=False):
                for kind, n in steps:
                    if kind in PANELS:
                        h = n % NH
                        if kind not in "cb" or h == 1:
                            act.wait_ge(proj_done, unit_of(i, kind, n, after) + 1)
                        if kind == "q":
                            for c in range(2):
                                ins = nc.scalar.activation(q_st[c][own[c], half_cols[h]], psum[own[c], h], ACT.Copy)
                            ins.then_inc(qk_hi, 1)
                        elif kind == "k":
                            for c in range(2):
                                for rows in (own[c], other[c]):
                                    ins = nc.scalar.activation(k_st[c][rows, half_cols[h]], psum[own[c], h], ACT.Copy)
                            ins.then_inc(qk_hi, 1)
                        elif kind == "v":
                            wait(act, a_ready, i * QB)
                            nc.scalar.activation(vt[:, half_cols[h]], psum[:, h], ACT.Copy).then_inc(vt_ready, 1)
                        elif kind == "h":
                            nc.scalar.activation(inner[:, 1 + h * HALF:1 + (h + 1) * HALF], psum[:, h], ACT.Copy
                                                 ).then_inc(h_ready, 1)
                        elif kind == "g":
                            if n == 0:
                                act.wait_ge(bias_ready, i + 1)
                            wait(act, gate_stored[h], i * (16 * GATE_PANELS) + 16 * (n // 2))
                            nc.scalar.activation(staging[h][:], psum[:, h], ACT.Tanh, scale=0.5,
                                                 bias=gate_bias[:, n // 2:n // 2 + 1]).then_inc(gate_ready, 1)
                            act.wait_ge(gate_ready, i * GATE_UNITS + (n + 1))
                            act.dma_start(one(gates.rearrange("b k p s -> p (b k) s"), i * GATE_PANELS + n // 2)
                                          [:, half_cols[h]], staging[h][:]).then_inc(gate_stored[h], 16)
                        if h == 1:
                            split_hi(*panel_of(i, kind, n, after, RING))
                    elif kind in "XM":
                        c = "MX".index(kind)
                        act.wait_ge(max_ready, i * (2 * QB) + (2 * n + 2 - c))
                        nc.scalar.activation(e[c][:], e[c][:], ACT.Exp, scale=SCALE, bias=neg_max[:, c:c + 1],
                                             accum_out=exp_sum[:, c:c + 1]).then_inc(exp_done, 1)
                    elif kind in ("VT", "T"):
                        act.wait_ge(tb_done, tb_use(i, kind, n) + 1)
                        dst = v_hl[0][:] if kind == "VT" else at_hl[0][:, :, (n % 4) * P:(n % 4 + 1) * P]
                        nc.scalar.activation(dst, tb_tiles, ACT.Copy).then_inc(tb_hi, 1)
                    elif kind == "AV":
                        wait(act, o_scaled, i * 2 - n)
                        act.wait_ge(tb_done, tb_use(i, kind, n) + 1)
                        nc.scalar.activation(dev[:], psum[:, TBK], ACT.Square).then_inc(osq_ready, 1)
                    elif kind == "O":
                        act.wait_ge(tb_done, tb_use(i, kind, n) + 1)
                        nc.scalar.activation(dev[:], psum[:, TBK], ACT.Sqrt, bias=eps, scale=1.0 / (2 * HD)
                                             ).then_inc(tb_free, 1)
                    elif kind == "ZS":
                        act.wait_ge(z_ready, NH * HEADS)
                        act.wait_ge(s_read, QB * HEADS)
                        nc.scalar.activation(z_hl[0][:, n], z[:, n], ACT.Copy).then_inc(zhi_ready, 1)
                    elif kind == "OS":
                        act.wait_ge(tb_free, HEADS * TB_USES)
                        act.wait_ge(o_scaled, 2 * n + 2)
                        nc.scalar.activation(o_hl[0][:, n], o[:, n], ACT.Copy).then_inc(ohi_ready, 1)

            walk(0, FIRST_TURN)
            with act.Fori(1, HEADS) as i:
                walk(i, TURN)
            for n, steps in enumerate(AFTER):
                walk(HEADS + n, steps, True)
            nc.scalar.preload_act_table(ACT.Tanh)
            with act.Fori(HEADS + len(AFTER), GATE_TURNS) as i:
                walk(i, [("g", n) for n in range(GATE_UNITS)], True)
            nc.scalar.preload_act_table(ACT.Sqrt)

            with act.Fori(0, KT // RING) as i:
                for j in range(RING):
                    act.wait_ge(br_done, i * (4 * RING) + (4 * j + 4))
                    split_hi(i * RING + (P_BR + j + RING), j, i + (P_BR + j + RING) // RING)
            def w_o_square(slot, number):
                act.wait_ge(wo_done, number + 1)
                act.wait_ge(msq_added, number + 1)
                nc.scalar.activation(relu[slot][:], psum[:, slot], ACT.Square).then_inc(msq_ready, 1)

            def split_next(panel):
                if panel + RING < P_END:
                    split_hi(panel + RING, panel % RING, panel // RING + 1)

            with act.Fori(0, KT // RING) as i:
                for j in range(RING):
                    w_o_square(j, i * RING + j)
                    split_hi(i * RING + (P_WO + j + RING), j, i + (P_WO + j + RING) // RING)

            def relu_squared_unit(bank, unit, hidden, slot, next_split=None):
                act.wait_ge(ff_done, unit + 1)
                wait(act, f_ready, hidden - 1)
                nc.scalar.activation(relu[slot][:], psum[:, bank], ACT.Relu).then_inc(relu_done, 1)
                act.wait_ge(relu_done, hidden + 1)
                nc.scalar.activation(relu[slot][:], relu[slot][:], ACT.Square).then_inc(relu_squared, 1)
                if next_split:
                    next_split()

            def deviation(n):
                wait(act, inv_ready, n)
                nc.scalar.activation(tok_dev, psum[:, SUM_BANK, 0:TILES_HALF], ACT.Sqrt, bias=eps, scale=1.0 / D
                                     ).then_inc(dev_ready, 1)

            def walk2(items):
                for kind, *where in items:
                    if kind == "W":
                        n, = where
                        w_o_square(n % RING, KT + n)
                        split_next(P_WO + KT + n)
                    elif kind == "MS":
                        h, = where
                        act.wait_ge(msum_done, h + 1)
                        deviation(2 * h)
                    elif kind == "B":
                        n, = where
                        act.wait_ge(spread_done, n + 1)
                        nc.scalar.activation(rstd[:], psum[:, SUM_BANK], ACT.Copy).then_inc(rstd_ready, 1)
                    elif kind == "R":
                        h, kt = where
                        act.wait_ge(h_sum_ready, h * KT + kt + 1)
                        squares(h * KT + kt, m[:, kt, half_cols[h]])
                    elif kind == "HS":
                        h, = where
                        act.wait_ge(sq_summed, (h + 1) * KT)
                        deviation(2 * h + 1)
                    elif kind == "U":
                        h, kt = where
                        act.wait_ge(u2_scaled, h * KT + kt + 1)
                        nc.scalar.activation(act_hl[0][:, kt, half_cols[h]], staging[kt % 2][:], ACT.Copy
                                             ).then_inc(u2_hi, 1)
                    elif kind == "F1":
                        c, h, j = where
                        if c + h + j == 0:
                            act.wait_ge(msq_added, NH + NH * KT)
                        relu_squared_unit(FF_BANKS[j % BANKS], c * FF_UNITS + h * (FFC + KT) + j,
                                          c * FF1_UNITS + h * FFC + j, j % 2,
                                          lambda: split_next(ff_panel(c, h, "F1", j)))
                    elif kind == "F2":
                        c, h, k = where
                        if k % 2 == 1:
                            act.wait_ge(ff_done, c * FF_UNITS + h * (FFC + KT) + FFC + k + 1)
                            split_next(ff_panel(c, h, "F2", k))
                    elif kind == "YS":
                        h, kt = where
                        act.wait_ge(acc_done, LAST * FF2_UNITS + h * KT + kt + 1)
                        squares((NH + h) * KT + kt, acc[:, h, kt])
                    elif kind == "YN":
                        h, = where
                        act.wait_ge(sq_summed, (NH + h + 1) * KT)
                        deviation(2 * NH + h)
                    elif kind == "YT":
                        _, t = where
                        act.wait_ge(yt_done[0], t + 1)
                        wait(act, stored0, 16 * t)
                        nc.scalar.activation(ost0[:, 0:HALF], psum[:, 2], ACT.Copy).then_inc(ost0_ready, 1)

            walk2(MIDDLE)
            with act.Fori(1, LAST) as i:
                for j in range(FF_PANELS):
                    nxt = (i * FF_PANELS + (P_LOOP + j + RING), j % RING,
                           i * (FF_PANELS // RING) + (P_LOOP + j + RING) // RING)
                    if j < FFC:
                        for h in range(NH):
                            u = NH * j + h
                            relu_squared_unit(FF_BANKS[u % BANKS], i * FF_UNITS + u, i * FF1_UNITS + u, h,
                                              (lambda: split_hi(*nxt)) if h == 1 else None)
                    else:
                        act.wait_ge(ff_done, i * FF_UNITS + (FF1_UNITS + 4 * (j - FFC) + 4))
                        split_hi(*nxt)
            walk2(END)
            act.wait_ge(yt_done[1], KT // 2)
            for t in range(TILES_HALF):
                nc.scalar.activation(ost1[t][:, 0:HALF], psum[:, 2 * t], ACT.Copy).then_inc(ost1_act, 1)
            act.wait_ge(yt_done[1], KT)
            for t in range(0, TILES_HALF, 2):
                nc.scalar.activation(ost1[t][:, HALF:D], psum[:, 2 * t + 1], ACT.Copy).then_inc(ost1_act, 1)

        @block.vector
        def _(dve):
            vec = nc.vector

            def lo_part(dst_hl, idx, src, semaphore, gain=None):
                hi, lo = dst_hl[0][idx].bitcast(F32), dst_hl[1][idx]
                if gain is None:
                    return vec.tensor_tensor(lo, src, hi, ALU.subtract).then_inc(semaphore, 1)
                return vec.scalar_tensor_tensor(out=lo, in0=src, scalar=gain, in1=hi, op0=ALU.mult,
                                                op1=ALU.subtract).then_inc(semaphore, 1)

            def split_lo(panel, slot):
                dve.wait_ge(w_hi, panel + 1)
                vec.tensor_tensor(w_hl[slot][1][:], w_raw[slot][:], w_hl[slot][0][:].bitcast(F32), ALU.subtract
                                  ).then_inc(w_split, 1)

            vec.memset(eps, EPS).then_inc(vec_setup, 1)

            def row_sum(t):
                dve.wait_ge(x_landed[t], 16)
                wait(dve, row_sums[1], t // 2)
                vec.tensor_tensor_reduce(out=xsq[1][:], in0=xn[:, t], in1=xn[:, t], scale=1.0, scalar=0.0,
                                         op0=ALU.mult, op1=ALU.add, accum_out=stats[:, t:t + 1]
                                         ).then_inc(row_sums[1], 1)

            def scale_rows(h):
                dve.wait_ge(row_dev, h + 1)
                cols = slice(TT + 4 * h, TT + 4 * h + 4)
                vec.reciprocal(stats[:, cols], stats[:, cols]).then_inc(row_rstd, 1)
                dve.wait_ge(row_rstd, h + 1)
                for t in range(4 * h, 4 * h + 4):
                    vec.tensor_scalar(xn[:, t], xn[:, t], stats[:, TT + t:TT + t + 1], None, ALU.mult
                                      ).then_inc(xn_ready, 1)

            def u_lo_parts(h):
                for kt in range(KT):
                    n = h * KT + kt
                    dve.wait_ge(u_hi, n + 1)
                    lo_part(act_hl, (slice(None), kt, half_cols[h]), psum[:, SB + n % 4], u_ready,
                            par[:, PAR_G + kt:PAR_G + kt + 1])

            row_sum(1)
            row_sum(3)
            dve.wait_ge(par_t, 1)
            vec.tensor_copy(par[:, 0:NPAR], psum[:, 7, 0:NPAR]).then_inc(par_ready, 1)
            scale_rows(0)
            split_lo(0, 0)
            row_sum(5)
            u_lo_parts(0)
            row_sum(7)
            scale_rows(1)
            u_lo_parts(1)
            dve.wait_ge(lqk_landed, 16)
            for c in range(2):
                wait(dve, dots_ready, c)
                vec.tensor_tensor_reduce(out=lq_junk[:], in0=lqk[:, 2 * c], in1=lqk[:, 2 * c + 1], scale=1.0,
                                         scalar=0.0, op0=ALU.mult, op1=ALU.add, accum_out=dots[:, c:c + 1]
                                         ).then_inc(dots_ready, 1)
            split_lo(1, 1)
            dve.wait_ge(par_ready, 1)
            vec.tensor_scalar(sub_gain, par[:, PAR_S:NPAR], 1.0 - LAM_INIT, None, ALU.mult).then_inc(vec_setup, 1)
            dve.wait_ge(setup, 5)
            vec.scalar_tensor_tensor(out=table[:], in0=table[:], scalar=-1.0, in1=table[:], op0=ALU.mult,
                                     op1=ALU.min).then_inc(vec_setup, 1)
            dve.wait_ge(vec_setup, 3)
            vec.tensor_scalar(table[:], table[:], SLOPES[0] / SCALE, None, ALU.mult).then_inc(table_ready, 1)
            dve.wait_ge(dot_exp_ready, 1)
            vec.tensor_tensor(lam_diff, dot_exp[:, 1:2], dot_exp[:, 0:1], ALU.subtract).then_inc(vec_setup, 1)
            dve.wait_ge(vec_setup, 4)
            vec.tensor_scalar(neg_lam, lam_diff, -LAM_INIT, None, ALU.add).then_inc(vec_setup, 1)

            def walk(i, steps, after=False):
                for kind, n in steps:
                    if kind in PANELS:
                        h = n % NH
                        u = unit_of(i, kind, n, after)
                        cols = half_cols[h]
                        if kind in "qk":
                            dve.wait_ge(qk_hi, i * 4 + (2 * "qk".index(kind) + h + 1))
                            for c in range(2):
                                hi = (q_st if kind == "q" else k_st)[c][own[c], cols].bitcast(F32)
                                lo = q_st[c][other[c], cols] if kind == "q" else k_lo[own[c], cols]
                                ins = vec.tensor_tensor(lo, psum[own[c], h], hi, ALU.subtract)
                            ins.then_inc(qk_ready, 1)
                        elif kind == "c":
                            dve.wait_ge(proj_done, u + 1)
                            dve.wait_ge(h_ready, i * 2 + (h + 1))
                            span = inner[:, 1 + h * HALF:1 + (h + 1) * HALF]
                            vec.tensor_tensor(span, psum[:, h], span, ALU.mult).then_inc(c_ready, 1)
                            if h == 1:
                                for tap in range(CONV_K):
                                    wc = par[:, bass.ds(i + (PAR_C + tap * CT), 1)]
                                    win = inner[:, tap:tap + S]
                                    if tap == 0:
                                        dve.wait_ge(c_ready, i * 2 + 2)
                                        vec.tensor_scalar(one(z, i), win, wc, None, ALU.mult).then_inc(taps, 1)
                                    else:
                                        dve.wait_ge(taps, i * CONV_K + tap)
                                        vec.scalar_tensor_tensor(out=one(z, i), in0=win, scalar=wc, in1=one(z, i),
                                                                 op0=ALU.mult, op1=ALU.add).then_inc(taps, 1)
                        elif kind == "b":
                            dve.wait_ge(proj_done, u + 1)
                            dve.wait_ge(taps, i * CONV_K + CONV_K)
                            vec.tensor_tensor(one(z, i)[:, cols], psum[:, h], one(z, i)[:, cols], ALU.mult
                                              ).then_inc(z_ready, 1)
                        if (kind, n) == (("g", 0) if after else ("c", 0)):
                            wait(dve, gate_ready, i * GATE_UNITS)
                            vec.tensor_scalar(gate_bias[:], par[:, bass.ds(i * GATE_PANELS + PAR_B, GATE_PANELS)], 0.5,
                                              None, ALU.mult).then_inc(bias_ready, 1)
                        if h == 1:
                            split_lo(*panel_of(i, kind, n, after, RING)[:2])
                    elif kind in "XM":
                        c = "MX".index(kind)
                        if (kind, n) == ("X", 0) and not isinstance(i, int):
                            vec.tensor_scalar(table[:], table[:], SLOPES[1] / SLOPES[0], None, ALU.mult
                                              ).then_inc(table_ready, 1)
                        if (kind, n) == ("X", 0):
                            dve.wait_ge(table_ready, i + 1)
                        if kind == "X":
                            dve.wait_ge(s_done, i * QB + (n + 1))
                            if n > 0:
                                dve.wait_ge(a_ready, i * QB + n)
                        elif n > 0:
                            dve.wait_ge(tb_done, tb_use(i, "T", n - 1) + 1)
                        vec.memset(spare, 0.0)
                        start = S - P - P * n
                        read = (s_read, map1_read)[c]
                        vec.tensor_tensor_reduce(
                            out=e[c][:], in0=psum[:, SB + 2 * c:SB + 2 * c + 2].rearrange("p b c -> p (b c)"),
                            in1=table[:, start:start + S], scale=1.0, scalar=-3.0e38, op0=ALU.add, op1=ALU.max,
                            accum_out=maxima[:, c:c + 1]).then_inc(read, 1)
                        dve.wait_ge(read, i * QB + (n + 1))
                        vec.tensor_scalar(neg_max[:, c:c + 1], maxima[:, c:c + 1], -SCALE, None, ALU.mult
                                          ).then_inc(max_ready, 1)
                    elif kind == "C":
                        blk = i * QB + (n if n < 7 else -1)
                        dve.wait_ge(exp_done, blk * 2 + 2)
                        vec.reciprocal(recip, exp_sum).then_inc(combine, 1)
                        dve.wait_ge(combine, blk * 3 + 1)
                        vec.tensor_scalar(weight2, recip[:, 1:2], neg_lam, None, ALU.mult).then_inc(combine, 1)
                        dve.wait_ge(combine, blk * 3 + 2)
                        vec.tensor_scalar(e[1][:], e[1][:], weight2, None, ALU.mult).then_inc(combine, 1)
                        dve.wait_ge(combine, blk * 3 + 3)
                        vec.scalar_tensor_tensor(out=e[0][:], in0=e[0][:], scalar=recip[:, 0:1], in1=e[1][:],
                                                 op0=ALU.mult, op1=ALU.add).then_inc(a_ready, 1)
                    elif kind in ("VT", "TL"):
                        dve.wait_ge(tb_hi, i * (QB + 1) + {"VT": 1, "TL": 2 + n if n < 7 else 0}[kind])
                        if kind == "VT":
                            lo_part(v_hl, slice(None), tb_tiles, tb_free)
                        else:
                            lo_part(at_hl, (slice(None), slice(None), slice((n % 4) * P, (n % 4 + 1) * P)), tb_tiles,
                                    tb_free)
                    elif kind == "AV":
                        dve.wait_ge(osq_ready, i * 2 - n + 1)
                        vec.tensor_scalar(one(o, i - n)[:, half_cols[n]], psum[:, TBK], 1.0, None, ALU.mult
                                          ).then_inc(tb_free, 1)
                    elif kind == "O":
                        k = i * 2 + (n - 2)
                        dve.wait_ge(tb_free, tb_use(i, kind, n) + 1)
                        vec.reciprocal(dev[:], dev[:]).then_inc(orstd_ready, 1)
                        dve.wait_ge(orstd_ready, k + 1)
                        span = one(o, i - 1)[:, half_cols[n]]
                        vec.scalar_tensor_tensor(out=span, in0=span, scalar=sub_gain, in1=dev[:], op0=ALU.mult,
                                                 op1=ALU.mult).then_inc(o_scaled, 1)
                    elif kind == "ZS":
                        dve.wait_ge(zhi_ready, n + 1)
                        lo_part(z_hl, (slice(None), n), z[:, n], zlo_ready)
                    elif kind == "OS":
                        dve.wait_ge(ohi_ready, n + 1)
                        lo_part(o_hl, (slice(None), n), o[:, n], olo_ready)

            walk(0, FIRST_TURN)
            with dve.Fori(1, HEADS) as i:
                walk(i, TURN)
            for n, steps in enumerate(AFTER):
                walk(HEADS + n, steps, True)
            with dve.Fori(HEADS + len(AFTER), GATE_TURNS) as i:
                walk(i, [("g", n) for n in range(GATE_UNITS)], True)

            with dve.Fori(0, KT // RING) as i:
                for j in range(RING):
                    for h in range(NH):
                        n = NH * j + h
                        for br in range(2):
                            if br == 0:
                                dve.wait_ge(gate_landed[h], i * (16 * RING) + 16 * (j + 1))
                            dve.wait_ge(br_done, i * (4 * RING) + (2 * n + br + 1))
                            vec.scalar_tensor_tensor(out=prod[br][:], in0=gate_in[h][:, br], scalar=1.0,
                                                     in1=psum[:, 2 * h + br], op0=ALU.add, op1=ALU.mult
                                                     ).then_inc(br_read, 1)
                            if br == 1 and h == 1:
                                split_lo(i * RING + (P_BR + j + RING), j)
                        dve.wait_ge(br_read, i * (4 * RING) + (4 + 2 * n + 2))
                        vec.tensor_tensor(prod[2][:], prod[0][:], prod[1][:], ALU.add).then_inc(merge_steps, 1)
                        hi = one(act_hl[0], i * RING + j)[:, half_cols[h]]
                        lo = one(act_hl[1], i * RING + j)[:, half_cols[h]]
                        dve.wait_ge(merge_steps, i * (4 * RING) + (2 * n + 1))
                        vec.tensor_scalar(hi, prod[2][:], 0.5, None, ALU.mult).then_inc(merge_steps, 1)
                        dve.wait_ge(merge_steps, i * (4 * RING) + (2 * n + 2))
                        vec.scalar_tensor_tensor(out=lo, in0=prod[2][:], scalar=0.5, in1=hi.bitcast(F32),
                                                 op0=ALU.mult, op1=ALU.subtract).then_inc(merged_ready, 1)
            def w_o_copy(slot, number, kt, h):
                dve.wait_ge(msq_ready, number + 1)
                vec.tensor_scalar(one(m, kt)[:, half_cols[h]], psum[:, slot], 1.0, None, ALU.mult
                                  ).then_inc(m_ready, 1)

            def split_next(panel):
                if panel + RING < P_END:
                    split_lo(panel + RING, panel % RING)

            with dve.Fori(0, KT // RING) as i:
                for j in range(RING):
                    w_o_copy(j, i * RING + j, i * RING + j, 0)
                    split_lo(i * RING + (P_WO + j + RING), j)

            def inverse(n):
                dve.wait_ge(dev_ready, n + 1)
                vec.reciprocal(tok_inv, tok_dev).then_inc(inv_ready, 1)
                dve.wait_ge(inv_ready, n + 1)
                if n == 0:
                    dve.wait_ge(o_scaled, HEADS * NH)
                else:
                    dve.wait_ge(spread_done, n)
                for t in range(TILES_HALF):
                    ins = vec.tensor_scalar(dev[:, t * P:(t + 1) * P], ident[:], tok_inv[:, t:t + 1], None, ALU.mult)
                ins.then_inc(diag_ready, 1)

            def scale_by(out_ap, in_ap, norm, kt, semaphore):
                col = PAR_G + norm * KT + kt
                vec.scalar_tensor_tensor(out=out_ap, in0=in_ap, scalar=par[:, col:col + 1], in1=rstd[:],
                                         op0=ALU.mult, op1=ALU.mult).then_inc(semaphore, 1)

            def split_f(slot, hidden, j, h):
                dve.wait_ge(relu_squared, hidden + 1)
                vec.tensor_copy(f_hl[0][:, j, half_cols[h]], relu[slot][:]).then_inc(fhi_ready, 1)
                dve.wait_ge(fhi_ready, hidden + 1)
                lo_part(f_hl, (slice(None), j, half_cols[h]), relu[slot][:], f_ready)

            def walk2(items):
                for kind, *where in items:
                    if kind == "W":
                        n, = where
                        w_o_copy(n % RING, KT + n, n, 1)
                    elif kind == "MS":
                        h, = where
                        inverse(2 * h)
                    elif kind == "B":
                        n, = where
                        dve.wait_ge(rstd_ready, n + 1)
                    elif kind == "R":
                        h, kt = where
                        n = h * KT + kt
                        span = m[:, kt, half_cols[h]]
                        if kt == 0:
                            dve.wait_ge(m_ready, 2 + (h + 1) * KT)
                        scale_by(span, span, 1, kt, m_scaled)
                        dve.wait_ge(m_scaled, n + 1)
                        dve.wait_ge(res_done, n + 1)
                        vec.tensor_tensor(span, psum[:, RES_BANKS[h][kt % len(RES_BANKS[h])]], span, ALU.add).then_inc(h_sum_ready, 1)
                    elif kind == "HS":
                        h, = where
                        inverse(2 * h + 1)
                        dve.wait_ge(h_sum_ready, (h + 1) * KT)
                    elif kind == "U":
                        h, kt = where
                        n = h * KT + kt
                        if kt == 0:
                            dve.wait_ge(sq_summed, n + KT)
                        wait(dve, u2_ready, n - 1)
                        scale_by(staging[n % 2][:], m[:, kt, half_cols[h]], 2, kt, u2_scaled)
                        for k in ([kt - 1] if kt > 0 else []) + ([kt] if kt == KT - 1 else []):
                            dve.wait_ge(u2_hi, h * KT + k + 1)
                            lo_part(act_hl, (slice(None), k, half_cols[h]), staging[k % 2][:], u2_ready)
                    elif kind == "F1":
                        c, h, j = where
                        split_f(j % 2, c * FF1_UNITS + h * FFC + j, j, h)
                        if c > 0:
                            split_next(ff_panel(c, h, "F1", j))
                    elif kind == "F2":
                        c, h, k = where
                        dve.wait_ge(ff_done, c * FF_UNITS + h * (FFC + KT) + FFC + k + 1)
                        bank = psum[:, FF_BANKS[k % BANKS]]
                        if c == 0:
                            vec.tensor_copy(acc[:, h, k], bank).then_inc(acc_done, 1)
                        else:
                            dve.wait_ge(acc_done, c * FF2_UNITS)
                            vec.tensor_tensor(acc[:, h, k], bank, acc[:, h, k], ALU.add).then_inc(acc_done, 1)
                        if k % 2 == 1 and c > 0:
                            split_next(ff_panel(c, h, "F2", k))
                    elif kind == "YN":
                        h, = where
                        inverse(2 * NH + h)
                        dve.wait_ge(acc_done, LAST * FF2_UNITS + (h + 1) * KT)
                    elif kind == "Y":
                        h, kt = where
                        scale_by(acc[:, h, kt], acc[:, h, kt], 3, kt, y_scaled)
                        if y_adder(h, kt)[0] == 0:
                            dve.wait_ge(y_scaled, h * KT + kt + 1)
                            span = m[:, kt, half_cols[h]]
                            vec.tensor_tensor(span, span, acc[:, h, kt], ALU.add).then_inc(y_ready[0], 1)
                    elif kind == "YT":
                        _, t = where
                        dve.wait_ge(yt_done[0], t + 1)
                        wait(dve, stored0, 16 * t)
                        vec.tensor_copy(ost0[:, HALF:D], psum[:, 3]).then_inc(ost0_ready, 1)

            walk2(MIDDLE)
            dve.wait_ge(w_split, FF_PANELS + P_LOOP + RING)
            with dve.Fori(1, LAST) as i:
                for j in range(FF_PANELS):
                    nxt = (i * FF_PANELS + (P_LOOP + j + RING), j % RING)
                    if j < FFC:
                        for h in range(NH):
                            split_f(h, i * FF1_UNITS + (NH * j + h), j, h)
                            if h == 1:
                                split_lo(*nxt)
                    else:
                        for dd in range(2):
                            for h in range(NH):
                                u = 4 * (j - FFC) + 2 * dd + h
                                dve.wait_ge(ff_done, i * FF_UNITS + (FF1_UNITS + u + 1))
                                dve.wait_ge(acc_done, i * FF2_UNITS)
                                span = acc[:, h, 2 * (j - FFC) + dd]
                                vec.tensor_tensor(span, psum[:, FF_BANKS[u % BANKS]], span, ALU.add
                                                  ).then_inc(acc_done, 1)
                                if dd == 1 and h == 1:
                                    split_lo(*nxt)
            walk2(END)
            dve.wait_ge(yt_done[1], KT)
            for t in range(1, TILES_HALF, 2):
                vec.tensor_copy(ost1[t][:, HALF:D], psum[:, 2 * t + 1]).then_inc(ost1_vec, 1)


NAMES = ["x", "w_in", "b_gate", "conv_w", "w_conv_out", "lambda_qk", "subln_g", "w_attn_out", "w_o", "norm_g",
         "w_ff1", "w_ff2"]


def kernel(**inputs):
    import numpy as np
    import concourse.bacc as bacc
    from concourse.bass_utils import run_bass_kernel_spmd

    nc = bacc.Bacc("TRN2", target_bir_lowering=False, num_devices=1)
    arrays, args = {}, []
    for name in NAMES:
        a = np.ascontiguousarray(inputs[name])
        arrays[f"in_{name}"] = a
        args.append(nc.dram_tensor(f"in_{name}", a.shape, mybir.dt.from_np(a.dtype), kind="ExternalInput").ap())
    args.append(nc.dram_tensor("out_0", (1, S, D), F32, kind="ExternalOutput").ap())
    build(nc, *args)
    r = run_bass_kernel_spmd(nc, [arrays], core_ids=[0])
    return r.results[0]["out_0"]
```
